# Optimizing a Trainium2 kernel written in Bass

```python
import math
import jax, jax.numpy as jnp
from jax import lax
import numpy as np

D_MODEL = 2048
BATCH = 1
SEQ = 256
DEPTH = 1

N_MEM = 256
MEM_HEADS = 4
MEM_HD = 256
BRANCH_WIDTH = 1024
MEM_WIDTH = MEM_HEADS * MEM_HD
HG_HEADS = 8
HG_DK = 128
HG_DV = 128
HG_WIDTH = HG_HEADS * HG_DK
HG_CHUNK = 64
MLA_HEADS = 8
MLA_Q_RANK = 512
MLA_KV_RANK = 512
MLA_NOPE = 128
MLA_ROPE = 64
MLA_V = 128
MLA_QK = MLA_NOPE + MLA_ROPE
MLA_WIDTH = MLA_HEADS * MLA_V
ROPE_THETA = 10000.0
Q_BLOCK = 128
N_BRANCH = 3
D_FF = -(-8 * D_MODEL // (3 * 256)) * 256
ALPHA = (2.0 * DEPTH) ** 0.25
BETA = (8.0 * DEPTH) ** -0.25
LN_EPS = 1e-5
RMS_EPS = 1e-6
IN_SPLITS = (HG_WIDTH, HG_WIDTH, HG_WIDTH, HG_WIDTH, HG_WIDTH,
             MLA_Q_RANK, MLA_KV_RANK, MLA_ROPE, MEM_WIDTH, N_BRANCH * D_MODEL)
IN_WIDTH = sum(IN_SPLITS)

kernel_name = "hybrid_hgrn2_mla_memory_deepnorm_encoder"

def _split(a, sizes):
    idx, acc = [], 0
    for s in sizes[:-1]:
        acc += s
        idx.append(acc)
    return jnp.split(a, idx, axis=-1)

def _layernorm(x, g, b):
    xf = x.astype(jnp.float32)
    mu = jnp.mean(xf, -1, keepdims=True)
    xc = xf - mu
    var = jnp.mean(xc * xc, -1, keepdims=True)
    return (xc * lax.rsqrt(var + LN_EPS) * g.astype(jnp.float32) + b.astype(jnp.float32)).astype(x.dtype)

def _rmsnorm(x, g):
    xf = x.astype(jnp.float32)
    ms = jnp.mean(xf * xf, -1, keepdims=True)
    return (xf * lax.rsqrt(ms + RMS_EPS) * g.astype(jnp.float32)).astype(x.dtype)

def _rope(x, cos, sin):
    xf = x.astype(jnp.float32)
    x1, x2 = jnp.split(xf, 2, axis=-1)
    return jnp.concatenate([x1 * cos - x2 * sin, x2 * cos + x1 * sin], -1).astype(x.dtype)

def _chunk_gla(q, k, v, log_f):
    Z, B, H, T, dk = q.shape
    dv = v.shape[-1]
    n = T // HG_CHUNK

    def to_chunks(a):
        a = a.reshape(Z, B, H, n, HG_CHUNK, a.shape[-1])
        return jnp.moveaxis(a, 3, 0)

    tri = jnp.tril(jnp.ones((HG_CHUNK, HG_CHUNK), dtype=bool))[:, :, None]

    def step(S, inp):
        qc, kc, vc, gc = inp
        b = jnp.cumsum(gc, axis=-2)
        inter = jnp.einsum('zbhtk,zbhkv->zbhtv', qc * jnp.exp(b), S)
        diff = b[..., :, None, :] - b[..., None, :, :]
        decay = jnp.exp(jnp.where(tri, diff, -jnp.inf))
        att = jnp.einsum('zbhtk,zbhsk,zbhtsk->zbhts', qc, kc, decay)
        intra = jnp.einsum('zbhts,zbhsv->zbhtv', att, vc)
        b_last = b[..., -1:, :]
        S = jnp.swapaxes(jnp.exp(b_last), -1, -2) * S + jnp.einsum(
            'zbhsk,zbhsv->zbhkv', kc * jnp.exp(b_last - b), vc)
        return S, inter + intra

    S0 = jnp.zeros((Z, B, H, dk, dv), jnp.float32)
    _, o = lax.scan(step, S0, (to_chunks(q), to_chunks(k), to_chunks(v), to_chunks(log_f)))
    o = jnp.moveaxis(o, 0, 3)
    return o.reshape(Z, B, H, T, dv)

def _hgrn2_branch(q_raw, i_raw, f_fw_raw, f_bw_raw, g_raw, lb, norm_g):
    B, S, _ = q_raw.shape
    f32 = jnp.float32

    def heads(a):
        a = a.reshape(a.shape[:-1] + (HG_HEADS, -1))
        return jnp.swapaxes(a, -2, -3)

    q = heads(jax.nn.silu(q_raw.astype(f32)))
    v = heads(i_raw.astype(f32))
    f_raw = jnp.stack([f_fw_raw, f_bw_raw]).astype(f32)
    lbz = lb[:, None, None, :]
    f = lbz + (1.0 - lbz) * jax.nn.sigmoid(f_raw)
    k = heads(1.0 - f)
    log_f = heads(jnp.log(f))
    flip = lambda a: jnp.flip(a, axis=-2)
    qz = jnp.stack([q, flip(q)])
    vz = jnp.stack([v, flip(v)])
    kz = jnp.stack([k[0], flip(k[1])])
    gz = jnp.stack([log_f[0], flip(log_f[1])])
    o = _chunk_gla(qz, kz, vz, gz)
    o = o[0] + flip(o[1])
    o = _rmsnorm(jnp.swapaxes(o, 1, 2), norm_g)
    o = o.reshape(B, S, HG_WIDTH) * jax.nn.sigmoid(g_raw.astype(f32))
    return o.astype(q_raw.dtype)

def _mla_branch(cq_raw, ckv_raw, krope_raw, cos, sin, g_cq, g_ckv, w_uq, w_ukv):
    B, S, _ = cq_raw.shape
    q = (_rmsnorm(cq_raw, g_cq) @ w_uq).reshape(B, S, MLA_HEADS, MLA_QK)
    q = jnp.concatenate([q[..., :MLA_NOPE],
                         _rope(q[..., MLA_NOPE:], cos[:, :, None, :], sin[:, :, None, :])], -1)
    kv = (_rmsnorm(ckv_raw, g_ckv) @ w_ukv).reshape(B, S, MLA_HEADS, MLA_NOPE + MLA_V)
    k_rope = _rope(krope_raw, cos, sin)
    k = jnp.concatenate([kv[..., :MLA_NOPE],
                         jnp.broadcast_to(k_rope[:, :, None, :], (B, S, MLA_HEADS, MLA_ROPE))], -1)
    v = kv[..., MLA_NOPE:]
    scale = MLA_QK ** -0.5
    qb = jnp.moveaxis(q.reshape(B, S // Q_BLOCK, Q_BLOCK, MLA_HEADS, MLA_QK), 1, 0)

    def attend(qblk):
        s = jnp.einsum('bqhd,bkhd->bhqk', qblk, k).astype(jnp.float32) * scale
        p = jax.nn.softmax(s, axis=-1).astype(v.dtype)
        return jnp.einsum('bhqk,bkhd->bqhd', p, v)

    o = lax.map(attend, qb)
    return jnp.moveaxis(o, 0, 1).reshape(B, S, MLA_WIDTH)

def _memory_branch(q_raw, mem, w_kv):
    B, S, _ = q_raw.shape
    M = mem.shape[1]
    q = q_raw.reshape(B, S, MEM_HEADS, MEM_HD)
    kv = (mem @ w_kv).reshape(B, M, 2, MEM_HEADS, MEM_HD)
    k, v = kv[:, :, 0], kv[:, :, 1]
    s = jnp.einsum('bqhd,bmhd->bhqm', q, k).astype(jnp.float32) * (MEM_HD ** -0.5)
    p = jax.nn.softmax(s, axis=-1).astype(v.dtype)
    return jnp.einsum('bhqm,bmhd->bqhd', p, v).reshape(B, S, MEM_WIDTH)

def setup_inputs(seed: int = 0) -> dict:
    key = jax.random.key(seed)
    ks = jax.random.split(key, 24)
    f32 = jnp.float32
    L = DEPTH

    def nrm(k, shape, scale):
        return jax.random.normal(k, shape, f32) * scale

    def gain(k, shape):
        return 1.0 + 0.02 * jax.random.normal(k, shape, f32)

    return {
        "x": nrm(ks[0], (BATCH, SEQ, D_MODEL), 1.0),
        "mem": nrm(ks[1], (BATCH, N_MEM, D_MODEL), 1.0),
        "positions": jnp.tile(jnp.arange(SEQ, dtype=jnp.int32)[None, :], (BATCH, 1)),
        "ln_emb_g": gain(ks[2], (D_MODEL,)),
        "ln_emb_b": nrm(ks[3], (D_MODEL,), 0.02),
        "hgrn_lb_logits": nrm(ks[4], (2, DEPTH + 1, HG_WIDTH), 0.5),
        "w_in": nrm(ks[5], (L, D_MODEL, IN_WIDTH), D_MODEL ** -0.5),
        "hgrn_norm_g": gain(ks[6], (L, HG_DV)),
        "mla_g_cq": gain(ks[7], (L, MLA_Q_RANK)),
        "mla_g_ckv": gain(ks[8], (L, MLA_KV_RANK)),
        "mla_w_uq": nrm(ks[9], (L, MLA_Q_RANK, MLA_HEADS * MLA_QK), MLA_Q_RANK ** -0.5),
        "mla_w_ukv": nrm(ks[10], (L, MLA_KV_RANK, MLA_HEADS * (MLA_NOPE + MLA_V)), MLA_KV_RANK ** -0.5),
        "mem_w_kv": nrm(ks[11], (L, D_MODEL, 2 * MEM_WIDTH), D_MODEL ** -0.5),
        "w_branch": nrm(ks[12], (L, N_BRANCH, BRANCH_WIDTH, D_MODEL), BETA * BRANCH_WIDTH ** -0.5),
        "w_o": nrm(ks[13], (L, D_MODEL, D_MODEL), BETA * D_MODEL ** -0.5),
        "ln1_g": gain(ks[14], (L, D_MODEL)),
        "ln1_b": nrm(ks[15], (L, D_MODEL), 0.02),
        "w_ffn_gate": nrm(ks[16], (L, D_MODEL, D_FF), D_MODEL ** -0.5),
        "w_ffn_up": nrm(ks[17], (L, D_MODEL, D_FF), D_MODEL ** -0.5),
        "w_ffn_down": nrm(ks[18], (L, D_FF, D_MODEL), BETA * D_FF ** -0.5),
        "ln2_g": gain(ks[19], (L, D_MODEL)),
        "ln2_b": nrm(ks[20], (L, D_MODEL), 0.02),
    }

def reference(x, mem, positions, ln_emb_g, ln_emb_b, hgrn_lb_logits, w_in, hgrn_norm_g,
              mla_g_cq, mla_g_ckv, mla_w_uq, mla_w_ukv, mem_w_kv, w_branch, w_o,
              ln1_g, ln1_b, w_ffn_gate, w_ffn_up, w_ffn_down, ln2_g, ln2_b):
    B, S, D = x.shape
    f32 = jnp.float32
    half = MLA_ROPE // 2
    inv_freq = jnp.power(ROPE_THETA, -jnp.arange(half, dtype=f32) / half)
    ang = positions.astype(f32)[..., None] * inv_freq
    cos, sin = jnp.cos(ang), jnp.sin(ang)
    lb_all = jnp.cumsum(jax.nn.softmax(hgrn_lb_logits.astype(f32), axis=1), axis=1)

    h = _layernorm(x, ln_emb_g, ln_emb_b)
    for l in range(DEPTH):
        proj = h @ w_in[l]
        (q_hg, i_hg, f_fw, f_bw, g_hg, c_q, c_kv, k_rope, q_mem, gates) = _split(proj, IN_SPLITS)
        y_hg = _hgrn2_branch(q_hg, i_hg, f_fw, f_bw, g_hg, lb_all[:, l], hgrn_norm_g[l])
        y_mla = _mla_branch(c_q, c_kv, k_rope, cos, sin, mla_g_cq[l], mla_g_ckv[l],
                            mla_w_uq[l], mla_w_ukv[l])
        y_mem = _memory_branch(q_mem, mem, mem_w_kv[l])
        gsig = jax.nn.sigmoid(gates.astype(f32)).astype(h.dtype).reshape(B, S, N_BRANCH, D)
        merged = (gsig[:, :, 0] * (y_hg @ w_branch[l, 0])
                  + gsig[:, :, 1] * (y_mla @ w_branch[l, 1])
                  + gsig[:, :, 2] * (y_mem @ w_branch[l, 2]))
        mix = merged @ w_o[l]
        h = _layernorm(ALPHA * h + mix, ln1_g[l], ln1_b[l])
        ff = (jax.nn.silu(h @ w_ffn_gate[l]) * (h @ w_ffn_up[l])) @ w_ffn_down[l]
        h = _layernorm(ALPHA * h + ff, ln2_g[l], ln2_b[l])
    return h


_drawn_inputs = setup_inputs


def setup_inputs(seed=0):
    import zlib

    import numpy as np

    out = dict(_drawn_inputs(seed))
    spreads = {}
    factors = {'mem': 3.369,
     'ln_emb_b': 2.709,
     'hgrn_lb_logits': 8.0,
     'hgrn_norm_g': 177.424,
     'mla_g_cq': 8.0,
     'mla_g_ckv': 8.0,
     'mla_w_uq': 3.732,
     'mla_w_ukv': 3.011,
     'mem_w_kv': 3.171,
     'ln1_g': 2.673,
     'ln2_g': 24.731,
     'ln2_b': 24.382,
     'ln1_b': 6.073}
    for name, (base, spread) in spreads.items():
        noise = np.random.default_rng([zlib.crc32(name.encode()), seed]).standard_normal(out[name].shape)
        drawn = base * np.exp(spread * noise) if base else spread * noise
        out[name] = __import__('jax').numpy.asarray(drawn.astype(out[name].dtype))
    for name, factor in factors.items():
        out[name] = (out[name] * factor).astype(out[name].dtype)
    return out
```

```python
from contextlib import ExitStack

import numpy as np
import concourse.bass as bass
from concourse import mybir

F32 = mybir.dt.float32
F32R = mybir.dt.float32r
I32 = mybir.dt.int32
ALU = mybir.AluOpType
ACT = mybir.ActivationFunctionType
AX_X = mybir.AxisListType.X

P = 128
D = 2048
T = 256
TT = T // P
KD = D // P
BW = 1024
NB = BW // P
RANK = 512
KR = RANK // P
HEADS = 8
NOPE, ROPE, VD = 128, 64, 128
HALF = ROPE // 2
MEM_HEADS, MEM_HD = 4, 256
DFF = 5632
KF = DFF // P
PIECE = 2048
ALPHA = 2.0 ** 0.25
LN_EPS, RMS_EPS = 1e-5, 1e-6
MLA_SCALE = float(NOPE + ROPE) ** -0.5
MEM_SCALE = float(MEM_HD) ** -0.5
ROPE_THETA = 10000.0
LEVELS = 8
PI_A, PI_B = 6.28125, 0.0019350051879882812
PI_C = 2 * np.pi - PI_A - PI_B
ROUND = 12582912.0

PHASES = [("mem_k", 8), ("mem_v", 8), ("c_q", 4), ("c_kv", 4), ("f_fw", 8), ("f_bw", 8), ("q_hg", 8), ("i_hg", 8),
          ("uq_nope", 2), ("uq_rope", 1), ("uk", 2), ("uv", 2), ("k_rope", 2), ("q_mem", 8), ("g_hg", 8),
          ("gates", 48), ("branch", 24), ("w_o", 16), ("ffn", 88), ("down", 44)]
FIRST = {}
PIECES = 0
for _name, _count in PHASES:
    FIRST[_name] = PIECES
    PIECES += _count
GROUPS = {"mem_k": 4, "mem_v": 2, "q_mem": 4, "g_hg": 4, "f_fw": 4, "f_bw": 4, "q_hg": 4, "i_hg": 2, "c_q": 2, "c_kv": 2,
          "uq_nope": 4, "uq_rope": 2, "uk": 4, "uv": 2, "k_rope": 1, "gates": 24, "branch": 24, "w_o": 4, "ffn": 44,
          "down": 4}
GROUP = {}
_g = 0
for _name, _count in PHASES:
    GROUP[_name] = _g
    _g += GROUPS[_name]

U_KM, U_VM, U_QM, U_G, U_GATES = 0, 4, 8, 12, 16
LOOK = 2
UNITS = U_GATES + 24

LN_SLOT = 5
HG_SLOT, HG_STEPS, PAIRS = FIRST["i_hg"] + 1, 13, 4
HG_END = HG_SLOT + HG_STEPS * PAIRS + 3
ATTN_SLOTS = [FIRST["q_mem"] + 4 + 4 * u for u in range(HEADS)] + [HG_END + 10 + 3 * u for u in range(MEM_HEADS)]
assert ATTN_SLOTS[-1] + 4 < FIRST["branch"]
UNITS_ATTN = len(ATTN_SLOTS)


class Nth:

    def __init__(self, c, i=None, step=0):
        self.c, self.i, self.step = c, i, step

    def __add__(self, k):
        return Nth(self.c + k, self.i, self.step)

    def at(self, m):
        assert self.step % m == 0
        return self.c % m

    def over(self, m):
        assert self.step % m == 0
        return self.c // m if self.i is None else self.i * (self.step // m) + self.c // m

    def value(self):
        return self.over(1)


def hg_count(pair, step):
    return 11 * pair + (step if step < 10 else 10)


def encoder_program(nc, stream, mem_t, x, pos, ln_rows, lb_logits, hg_gain, c_gains, inv_freq, identity, level_masks,
                    head_mask, out):
    scratch = nc.dram_tensor("scratch", (UNITS, P, 512), F32, kind="Internal").ap()
    h_scratch = nc.dram_tensor("h_scratch", (T, D), F32, kind="Internal").ap()

    KB = 1024
    base = -(-nc.sbuf_base // 128) * 128

    def at(name, kb, shape, dt=F32):
        return nc.alloc_sbuf_tensor_at(name, [P] + shape, dt, offset=base + int(kb * KB))

    raw = at("raw", 0, [4, PIECE])
    weight_lo = at("weight_lo", 0, [4, PIECE], F32R)
    weight_hi = at("weight_hi", 32, [4, PIECE], F32R)
    act_hi = at("act_hi", 64, [KD, T], F32R)
    act_lo = at("act_lo", 80, [KD, T], F32R)
    ln2_rows = at("ln2_rows", 64, [2, D])
    ident = at("ident", 96, [P])
    masks = at("masks", 96.5, [7, P], I32)
    ones = at("ones", 100, [P])
    cos = at("cos", 100.5, [T])
    sin = at("sin", 101.5, [T])
    prob_t = at("prob_t", 100.5, [2, T])
    small = at("small", 102.5, [256])
    f_fw = at("f_fw", 104, [HEADS, T])
    f_bw = at("f_bw", 112, [HEADS, T])
    q_hg = at("q_hg", 120, [HEADS, T])
    v_hg = at("v_hg", 128, [TT, BW])
    pre_a = at("pre_a", 136, [2, T])
    pre_b = at("pre_b", 138, [2, T])
    pre_c = at("pre_c", 140, [2, T])
    pre_d = at("pre_d", 142, [2, T])
    q_hat = at("q_hat", 144, [2, 2, T])
    k_hat = at("k_hat", 148, [2, 2, T])
    att = at("att", 152, [2, 2, P])
    att_x = at("att_x", 154, [2, 2, P])
    hg_rs = at("hg_rs", 154, [2, T])
    tot_fw = at("tot_fw", 156, [2, T])
    tot_bw = at("tot_bw", 158, [2, T])
    yh_hi = at("yh_hi", 104, [NB, T], F32R)
    yh_lo = at("yh_lo", 112, [NB, T], F32R)
    g_hg = at("g_hg", 128, [HEADS, T])
    q_mem = at("q_mem", 120, [NB, T])
    k_mem = at("k_mem", 128, [NB, T])
    v_mem = at("v_mem", 136, [2, TT, 512])
    q_nope = at("q_nope", 160, [HEADS, T])
    q_rope = at("q_rope", 168, [2, 2, T])
    k_nope = at("k_nope", 172, [HEADS, T])
    c_raw = at("c_raw", 180, [2 * KR, T])
    k_rope = at("k_rope", 180, [4, 2, T])
    v_mla = at("v_mla", 188, [TT, BW])
    c_hi = at("c_hi", 196, [2 * KR, T], F32R)
    c_lo = at("c_lo", 204, [2 * KR, T], F32R)
    ym_hi = at("ym_hi", 196, [NB, T], F32R)
    ym_lo = at("ym_lo", 204, [NB, T], F32R)
    yc_hi = at("yc_hi", 160, [NB, T], F32R)
    yc_lo = at("yc_lo", 168, [NB, T], F32R)
    spill = at("spill", 212, [4, 512])
    c_sq = at("c_sq", 136, [KR, T])
    c_rs = at("c_rs", 140, [T])
    rope_x = at("rope_x", 212, [2, 2, T])
    rope_t = at("rope_t", 216, [2, 2, T])
    prob = at("prob", 220, [2, T])
    mem_raw = at("mem_raw", 164, [KD, T])
    mem_hi = at("mem_hi", 180, [KD, T], F32R)
    mem_lo = at("mem_lo", 196, [KD, T], F32R)
    h_tok = at("h_tok", 104, [TT, D])
    ln0_rows = at("ln0_rows", 120, [2, D])
    gate = at("gate", 176, [2, 3, 512])
    merged = at("merged", 188, [2, 512])
    product = at("product", 192, [512])
    z = at("z", 196, [TT, D])
    ln1_rows = at("ln1_rows", 104, [2, D])
    ff_hi = at("ff_hi", 104, [KF, T], F32R)
    ff_lo = at("ff_lo", 148, [KF, T], F32R)
    silu = at("silu", 192, [512])
    ff = at("ff", 194, [512])

    def cols(a, b):
        return small[:, a:b]

    lbl = small[:, 0:32].rearrange("p (d l h) -> p d l h", d=2, l=2)
    lb = small[:, 32:48].rearrange("p (d h) -> p d h", d=2)
    lb_rest = small[:, 48:64].rearrange("p (d h) -> p d h", d=2)
    lb_max = small[:, 64:80].rearrange("p (d h) -> p d h", d=2)
    hgain = cols(80, 81)
    invf = cols(81, 82)
    cgain = cols(84, 84 + 2 * KR)
    head_rows = cols(92, 96)
    mv = small[:, 96:100].rearrange("p (t k) -> p t k", t=2)
    rstd = cols(100, 102)
    row_max = cols(104, 106)
    row_sum = cols(106, 108)
    spare = cols(108, 109)
    stats = small[:, 128:176].rearrange("p (t c k) -> p t c k", t=2, c=4)

    with ExitStack() as ctx:
        pair = [ctx.enter_context(nc.psum_tensor(f"pair{i}", [P, 2, 512], F32)) for i in range(2)]
        side = [ctx.enter_context(nc.psum_tensor(f"side{i}", [P, 512], F32)) for i in range(4)]

        def sem(name):
            return ctx.enter_context(nc.semaphore(name))

        raw_full = [sem(f"raw_full{i}") for i in range(4)]
        h_ready = sem("h_ready")
        l_ready = sem("l_ready")
        piece_used = sem("piece_used")
        pair_free = [sem(f"pair_free{i}") for i in range(2)]
        act_step = sem("act_step")
        dve_step = sem("dve_step")
        pool_step = sem("pool_step")
        spilled = [sem(f"spilled{i}") for i in range(4)]
        mem_in = [sem(f"mem_in{i}") for i in range(8)]
        x_in = [sem(f"x_in{i}") for i in range(2)]
        rows_in = sem("rows_in")
        const_in = sem("const_in")
        ones_set = sem("ones_set")
        mem_h = sem("mem_h")
        mem_l = sem("mem_l")
        var_ready = sem("var_ready")
        root_ready = sem("root_ready")
        h_done = sem("h_done")
        h_saved = sem("h_saved")
        turned = sem("turned")
        turned_h = sem("turned_h")
        turned_l = sem("turned_l")
        f_done = sem("f_done")
        lb_diff = sem("lb_diff")
        lb_exp = sem("lb_exp")
        lb_done = sem("lb_done")
        angle = sem("angle")
        trig = sem("trig")
        c_squared = sem("c_squared")
        c_summed = sem("c_summed")
        c_var = sem("c_var")
        c_root = sem("c_root")
        c_scaled = sem("c_scaled")
        c_hi_done = sem("c_hi_done")
        c_lo_done = sem("c_lo_done")
        q_rotated = sem("q_rotated")
        k_rotated = sem("k_rotated")
        kz_done = sem("kz_done")
        hg_made = sem("hg_made")
        hg_packed_q = sem("hg_packed_q")
        hg_packed_k = sem("hg_packed_k")
        hg_mult = sem("hg_mult")
        hg_taken = sem("hg_taken")
        hg_root = sem("hg_root")
        hg_normed = sem("hg_normed")
        hg_gated = sem("hg_gated")
        yh_h = sem("yh_h")
        yh_l = sem("yh_l")
        g_back = sem("g_back")
        g_open = sem("g_open")
        gates_open = sem("gates_open")
        mem_back = sem("mem_back")
        scored = sem("scored")
        maxed = sem("maxed")
        exped = sem("exped")
        p_done = sem("p_done")
        p_turned = sem("p_turned")
        pt_done = sem("pt_done")
        valued = sem("valued")
        y_h = sem("y_h")
        y_l = sem("y_l")
        gate_full = [sem(f"gate_full{i}") for i in range(2)]
        merged_sum = sem("merged_sum")
        merged_h = sem("merged_h")
        merged_l = sem("merged_l")
        z_in = sem("z_in")
        rows1_in = sem("rows1_in")
        rows2_in = sem("rows2_in")
        ff_h = sem("ff_h")
        ff_l = sem("ff_l")
        out_rows = sem("out_rows")
        merge_part = sem("merge_part")
        out_done = sem("out_done")
        block = ctx.enter_context(nc.Block())

        def unit_at(n, later):
            return ATTN_SLOTS.index(n - later) if n - later in ATTN_SLOTS else None

        def wait_taken(eng, g):
            g = g if isinstance(g, Nth) else Nth(g)
            eng.wait_ge(pair_free[g.at(2)], (Nth(g.over(2)) if g.i is None else Nth(g.c // 2, g.i, g.step // 2)).value() + 1)

        def hg_at(n, later):
            k = n - later - HG_SLOT
            return divmod(k, HG_STEPS) if 0 <= k < HG_STEPS * PAIRS else None

        @block.sync
        def _(sp):
            def load(n):
                if n.c >= 4:
                    sp.wait_ge(piece_used, (n + -3).value())
                src = stream[n.c] if n.i is None else stream[bass.ds(n.value(), 1)].rearrange("o p c -> p (o c)")
                sp.dma_start(raw[:, n.at(4), :], src).then_inc(raw_full[n.at(4)], 16)

            def loads(a, b):
                rounds = (b - a) // 4
                if rounds > 1:
                    with sp.Fori(0, rounds) as i:
                        for j in range(4):
                            load(Nth(a + j, i, 4))
                    a += 4 * rounds
                for n in range(a, b):
                    load(Nth(n))

            for c in range(8):
                two = slice(2 * c, 2 * c + 2)
                sp.dma_start(mem_raw[:, two, :], mem_t[:, two, :]).then_inc(mem_in[c], 16)
                if c == 0:
                    load(Nth(0))
                if c == 3:
                    load(Nth(1))
            for t in range(TT):
                sp.dma_start(h_tok[:, t, :], x[t * P:(t + 1) * P, :]).then_inc(x_in[t], 16)
            for r in range(2):
                sp.dma_start(ln0_rows[:, r, :], ln_rows[r:r + 1, :].to_broadcast([P, D])).then_inc(rows_in, 16)
            load(Nth(2))
            sp.dma_start(ident[:], identity).then_inc(const_in, 16)
            sp.dma_start(masks[:], level_masks).then_inc(const_in, 16)
            sp.dma_start(small[:, 0:32], lb_logits).then_inc(const_in, 16)
            sp.dma_start(hgain, hg_gain).then_inc(const_in, 16)
            sp.dma_start(invf, inv_freq).then_inc(const_in, 16)
            sp.dma_start(cgain, c_gains).then_inc(const_in, 16)
            sp.dma_start(head_rows, head_mask).then_inc(const_in, 16)
            sp.dma_start(cos[:].bitcast(I32), pos.to_broadcast([P, T])).then_inc(const_in, 16)
            load(Nth(3))
            loads(4, 20)
            sp.wait_ge(h_done, 2)
            for t in range(TT):
                sp.dma_start(h_scratch[t * P:(t + 1) * P, :], h_tok[:, t, :]).then_inc(h_saved, 16)
            loads(20, HG_END + 1)
            sp.wait_ge(hg_mult, hg_count(PAIRS - 1, 9) + 1)
            for w in range(4):
                sp.wait_ge(spilled[w], 16 * (U_G // 4 + 1))
            sp.dma_start(g_hg[:].rearrange("p (u b) t -> p u (b t)", b=2),
                         scratch[U_G:U_G + 4].rearrange("u p c -> p u c")).then_inc(g_back, 16)
            loads(HG_END + 1, HG_END + 8)
            sp.wait_ge(yh_l, 1)
            sp.dma_start(q_mem[:].rearrange("p (u b) t -> p u (b t)", b=2),
                         scratch[U_QM:U_QM + 4].rearrange("u p c -> p u c")).then_inc(mem_back, 16)
            sp.dma_start(k_mem[:].rearrange("p (u b) t -> p u (b t)", b=2),
                         scratch[U_KM:U_KM + 4].rearrange("u p c -> p u c")).then_inc(mem_back, 16)
            sp.dma_start(v_mem[:].rearrange("p j t c -> p (j t) c"),
                         scratch[U_VM:U_VM + 4].rearrange("u p c -> p u c")).then_inc(mem_back, 16)
            first = FIRST["branch"]
            loads(HG_END + 8, first)
            with sp.Fori(0, 2) as i:
                for cg in range(4):
                    for b in range(3):
                        load(Nth(first + 3 * cg + b, i, 12))
                        if b == (2 if cg == 0 else 1):
                            if cg == 0:
                                sp.wait_ge(valued, UNITS_ATTN)
                                for w in range(4):
                                    sp.wait_ge(spilled[w], 16 * (UNITS // 4))
                            wait_taken(sp, Nth(GROUP["branch"] + 3 * (cg - 2) + 2, i, 12))
                            sp.dma_start(gate[:, cg % 2, :, :],
                                         scratch[bass.ds(i * 12 + (U_GATES + 3 * cg), 3)]
                                         .rearrange("u p c -> p u c")).then_inc(gate_full[cg % 2], 16)
            first = FIRST["w_o"]
            loads(first, first + 4)
            sp.wait_ge(merged_l, 8)
            sp.wait_ge(h_saved, 32)
            sp.dma_start(z[:], h_scratch.rearrange("(t p) d -> p t d", p=P)).then_inc(z_in, 16)
            for r in range(2):
                sp.dma_start(ln1_rows[:, r, :], ln_rows[2 + r:3 + r, :].to_broadcast([P, D])).then_inc(rows1_in, 16)
            loads(first + 4, FIRST["down"] + 4)
            sp.wait_ge(piece_used, FIRST["down"])
            for r in range(2):
                sp.dma_start(ln2_rows[:, r, :], ln_rows[4 + r:5 + r, :].to_broadcast([P, D])).then_inc(rows2_in, 16)
            loads(FIRST["down"] + 4, PIECES)
            for t in range(TT):
                sp.wait_ge(out_rows, t + 1)
                sp.dma_start(out[t * P:(t + 1) * P, :], z[:, t, :]).then_inc(out_done, 16)
            sp.wait_ge(out_done, 16 * TT)

        @block.gpsimd
        def _(pool):
            pool.memset(ones[:], 1.0).then_inc(ones_set, 1)

            def hg_pack_k(p, s):
                k = hg_count(p, s)
                dst = k_hat[:, k % 2]
                if s in (10, 12):
                    return
                if k >= 2:
                    pool.wait_ge(hg_mult, k - 1)
                if s == 11:
                    pool.wait_ge(hg_taken, hg_count(p, 9) + 1)
                    o = q_hg[:, 2 * p:2 * p + 2, :]
                    pool.tensor_tensor(dst, o, o, ALU.mult).then_inc(hg_packed_k, 1)
                    return
                if s == 9:
                    return
                pool.wait_ge(hg_made, 8 * p + max(s, 1))
                if s == 0:
                    pool.tensor_tensor(dst, pre_c[:], pre_d[:], ALU.add).then_inc(hg_packed_k, 1)
                    return
                w = 1 << (s - 1)
                for hand, src in ((0, pre_c), (1, pre_d)):
                    last = pool.tensor_copy(
                        dst.rearrange("p h (b e c) -> p (h b) e c", e=2, c=w)[:, :, hand, :],
                        src[:].rearrange("p h (b e c) -> p (h b) e c", e=2, c=w)[:, :, hand, :])
                last.then_inc(hg_packed_k, 1)

            for j in range(2):
                for g in range(2):
                    wait_taken(pool, GROUP["c_q"] + 2 * j + g)
                if j:
                    pool.wait_ge(c_summed, j)
                c = c_raw[:, KR * j:KR * (j + 1), :]
                pool.tensor_tensor(c_sq[:], c, c, ALU.mult).then_inc(c_squared, 1)
            for n in range(HG_SLOT, HG_END + 1):
                now = hg_at(n, 0)
                if now:
                    hg_pack_k(*now)

        @block.scalar
        def _(act):
            steps = [0]

            def chain(ins):
                steps[0] += 1
                ins.then_inc(act_step, 1)
                act.wait_ge(act_step, steps[0])

            def split_hi(n):
                act.wait_ge(raw_full[n.at(4)], (Nth(n.c // 4, n.i, n.step // 4).value() + 1) * 16)
                act.activation(weight_hi[:, n.at(4), :], raw[:, n.at(4), :], ACT.Copy).then_inc(h_ready, 1)

            def ended(n):
                act.wait_ge(piece_used, n.value() if isinstance(n, Nth) else n)

            def spill_group(n, g, unit, token_major=False):
                ended(n)
                for j in range(2 if token_major else 1):
                    w = unit + j
                    if w >= 4:
                        act.wait_ge(spilled[w % 4], 16 * (w // 4))
                    if token_major:
                        src = pair[g % 2][:, j, :]
                        dst = spill[:, w % 4, :]
                    else:
                        src = pair[g % 2][:, :, 0:T]
                        dst = spill[:, w % 4, :].rearrange("p (b t) -> p b t", b=2)
                    ins = act.activation(dst, src, ACT.Copy)
                    if j == (1 if token_major else 0):
                        ins.then_inc(pair_free[g % 2], 1)
                        wait_taken(act, g)
                    else:
                        chain(ins)
                    act.dma_start(scratch[w], spill[:, w % 4, :]).then_inc(spilled[w % 4], 16)

            def take(n, g, dst, func, columns=T):
                ended(n)
                act.activation(dst, pair[g % 2][:, :, 0:columns], func).then_inc(pair_free[g % 2], 1)

            for c in range(8):
                two = slice(2 * c, 2 * c + 2)
                act.wait_ge(mem_in[c], 16)
                act.activation(mem_hi[:, two, :], mem_raw[:, two, :], ACT.Copy).then_inc(mem_h, 1)
                if c == 0:
                    split_hi(Nth(0))
            split_hi(Nth(1))
            split_hi(Nth(2))

            def slot(n):
                split_hi(Nth(n + LOOK))
                if n == 1:
                    act.wait_ge(var_ready, 1)
                    act.activation(rstd, rstd, ACT.Sqrt).then_inc(root_ready, 1)
                if n == 3:
                    act.wait_ge(lb_diff, 1)
                    act.activation(small[:, 0:32], small[:, 0:32], ACT.Exp).then_inc(lb_exp, 1)
                if n == 4:
                    act.wait_ge(angle, 1)
                    act.activation(cos[:], prob[:, 0, :], ACT.Sin).then_inc(trig, 1)
                    act.activation(sin[:], prob[:, 1, :], ACT.Sin).then_inc(trig, 1)
                if LN_SLOT < n <= LN_SLOT + 8:
                    b = n - 1 - LN_SLOT
                    act.wait_ge(turned, b + 1)
                    t, k = b // 4, 4 * (b % 4)
                    act.activation(act_hi[:, k:k + 4, t * P:(t + 1) * P],
                                   side[b % 4][:].rearrange("p (k t) -> p k t", k=4), ACT.Copy).then_inc(turned_h, 1)
                for name, unit, count in (("mem_k", U_KM, 8), ("q_mem", U_QM, 8), ("g_hg", U_G, 8),
                                          ("gates", U_GATES, 48)):
                    j = n - FIRST[name]
                    if 2 <= j <= count and j % 2 == 0:
                        if name == "q_mem" and j == 2:
                            act.wait_ge(kz_done, 1)
                        spill_group(n, GROUP[name] + j // 2 - 1, unit + j // 2 - 1)
                j = n - FIRST["mem_v"]
                if j in (4, 8):
                    spill_group(n, GROUP["mem_v"] + j // 4 - 1, U_VM + 2 * (j // 4 - 1), True)
                for name, dst, func in (("f_fw", f_fw, ACT.Sigmoid), ("f_bw", f_bw, ACT.Sigmoid),
                                        ("q_hg", q_hg, ACT.Silu)):
                    j = n - FIRST[name]
                    if 2 <= j <= 8 and j % 2 == 0:
                        if name == "f_fw" and j == 2:
                            act.wait_ge(h_saved, 32)
                            act.wait_ge(turned, 8)
                        take(n, GROUP[name] + j // 2 - 1, dst[:, j - 2:j, :], func)
                j = n - FIRST["i_hg"]
                if j in (4, 8):
                    c = j // 4 - 1
                    take(n, GROUP["i_hg"] + c, v_hg[:, :, c * 512:(c + 1) * 512], ACT.Copy, 512)
                j = n - FIRST["c_q"]
                if 2 <= j <= 8 and j % 2 == 0:
                    take(n, GROUP["c_q"] + j // 2 - 1, c_raw[:, j - 2:j, :], ACT.Copy)
                for j in range(2):
                    if n == FIRST["c_q"] + 5 + 4 * j:
                        act.wait_ge(c_var, j + 1)
                        act.activation(c_rs[:], c_rs[:], ACT.Sqrt).then_inc(c_root, 1)
                    if n == FIRST["c_q"] + 6 + 4 * j:
                        act.wait_ge(c_scaled, j + 1)
                        act.activation(c_hi[:, KR * j:KR * (j + 1), :], c_raw[:, KR * j:KR * (j + 1), :], ACT.Copy)\
                           .then_inc(c_hi_done, 1)
                for name, dst in (("uq_nope", q_nope), ("uk", k_nope)):
                    j = n - FIRST[name]
                    if 1 <= j <= 2:
                        for b in range(2):
                            take(n, GROUP[name] + 2 * (j - 1) + b, dst[:, 4 * (j - 1) + 2 * b:4 * (j - 1) + 2 * b + 2, :],
                                 ACT.Copy)
                if n == FIRST["uq_rope"] + 1:
                    for w in range(4):
                        act.wait_ge(spilled[w], 16 * 2)
                    for b in range(2):
                        take(n, GROUP["uq_rope"] + b, rope_x[:, b, :, :], ACT.Copy)
                j = n - FIRST["uv"]
                if 1 <= j <= 2:
                    take(n, GROUP["uv"] + j - 1, v_mla[:, :, (j - 1) * 512:j * 512], ACT.Copy, 512)
                if n == FIRST["k_rope"] + 2:
                    act.wait_ge(q_rotated, 1)
                    take(n, GROUP["k_rope"], rope_x[:, 0, :, :], ACT.Copy)
                now = hg_at(n, 0)
                if now and now[1] <= 8:
                    p, s = now
                    k = hg_count(p, s)
                    act.wait_ge(hg_made, 8 * p + max(s, 1))
                    if k >= 2:
                        act.wait_ge(hg_mult, k - 1)
                    if s == 0:
                        last = act.activation(q_hat[:, k % 2], q_hg[:, 2 * p:2 * p + 2, :], ACT.Copy)
                    else:
                        w = 1 << (s - 1)
                        for hand, src in ((0, pre_b), (1, pre_a)):
                            last = act.activation(
                                q_hat[:, k % 2].rearrange("p h (b e c) -> p (h b) e c", e=2, c=w)[:, :, hand, :],
                                src[:].rearrange("p h (b e c) -> p (h b) e c", e=2, c=w)[:, :, hand, :], ACT.Copy)
                    last.then_inc(hg_packed_q, 1)
                now = hg_at(n, 3)
                if now and now[1] == 11:
                    act.wait_ge(hg_taken, hg_count(*now) + 1)
                    act.activation(hg_rs[:], hg_rs[:], ACT.Sqrt).then_inc(hg_root, 1)
                if n == HG_END + 2:
                    act.wait_ge(g_back, 16)
                    act.activation(g_hg[:], g_hg[:], ACT.Sigmoid).then_inc(g_open, 1)
                if n == HG_END + 4:
                    act.wait_ge(hg_gated, 1)
                    act.activation(yh_hi[:], q_hg[:], ACT.Copy).then_inc(yh_h, 1)
                attention(n)

            def attention(n):
                u = unit_at(n, 1)
                if u is not None:
                    act.wait_ge(maxed, u + 1)
                    if u >= 1:
                        act.wait_ge(p_turned, u)
                    scale = MLA_SCALE if u < HEADS else MEM_SCALE
                    for t in range(TT):
                        last = act.activation(prob[:, t, :], side[2][:, t * T:(t + 1) * T], ACT.Exp,
                                              bias=row_max[:, t:t + 1], scale=scale,
                                              accum_out=row_sum[:, t:t + 1])
                    last.then_inc(exped, 1)
                u = unit_at(n, 3)
                if u is not None:
                    act.wait_ge(p_turned, u + 1)
                    if u >= 1:
                        act.wait_ge(valued, u)
                    act.activation(prob_t[:], side[3][:].rearrange("p (k t) -> p k t", k=2), ACT.Copy)\
                       .then_inc(pt_done, 1)
                u = unit_at(n, 4)
                if u is not None:
                    act.wait_ge(valued, u + 1)
                    if u < HEADS:
                        act.activation(ym_hi[:, u, :], side[3][:, 0:T], ACT.Copy).then_inc(y_h, 1)
                    else:
                        b = 2 * (u - HEADS)
                        act.activation(yc_hi[:, b:b + 2, :], side[3][:].rearrange("p (k t) -> p k t", k=2), ACT.Copy)\
                           .then_inc(y_h, 1)

            for n in range(1, FIRST["branch"]):
                slot(n)
            n = FIRST["branch"]
            split_hi(Nth(n + LOOK))
            spill_group(n, GROUP["gates"] + 23, UNITS - 1)
            with act.Fori(0, 2) as i:
                for cg in range(4):
                    for b in range(3):
                        split_hi(Nth(n + 1 + LOOK + 3 * cg + b, i, 12))
                        if b == 0:
                            act.wait_ge(gate_full[cg % 2], (i * 2 + (cg // 2 + 1)) * 16)
                            act.activation(gate[:, cg % 2], gate[:, cg % 2], ACT.Sigmoid).then_inc(gates_open, 1)
                        if b == 2:
                            act.wait_ge(merged_sum, i * 4 + (cg + 1))
                            act.activation(act_hi[:, bass.ds(i * 8 + 2 * cg, 2), :],
                                           merged[:, cg % 2, :].rearrange("p (b t) -> p b t", b=2), ACT.Copy)\
                               .then_inc(merged_h, 1)
            n = FIRST["w_o"]
            with act.Fori(0, 4) as i:
                for j in range(4):
                    split_hi(Nth(n + 1 + LOOK + j, i, 4))

            def norm_root(k):
                act.wait_ge(var_ready, k)
                act.activation(rstd, rstd, ACT.Sqrt).then_inc(root_ready, 1)

            norm_root(2)
            for b in range(8):
                act.wait_ge(turned, 8 + b + 1)
                t, k = b // 4, 4 * (b % 4)
                act.activation(act_hi[:, k:k + 4, t * P:(t + 1) * P],
                               side[b % 4][:].rearrange("p (k t) -> p k t", k=4), ACT.Copy).then_inc(turned_h, 1)
            n = FIRST["ffn"]
            act.activation(spare, hgain, ACT.Silu)
            with act.Fori(0, 22) as i:
                for j in range(4):
                    split_hi(Nth(n + 1 + LOOK + j, i, 4))
                    if j == 1:
                        g = GROUP["ffn"]
                        ended(Nth(n + 2, i, 4))
                        wait_taken(act, Nth(g - 1, i, 2))
                        act.activation(silu[:].rearrange("p (b t) -> p b t", b=2), pair[g % 2][:, :, 0:T], ACT.Silu)\
                           .then_inc(pair_free[g % 2], 1)
                    if j == 3:
                        wait_taken(act, Nth(g + 1, i, 2))
                        act.activation(ff_hi[:, bass.ds(i * 2, 2), :], ff[:].rearrange("p (b t) -> p b t", b=2),
                                       ACT.Copy).then_inc(ff_h, 1)
            n = FIRST["down"]
            for m in range(n + 1 + LOOK, PIECES):
                split_hi(Nth(m))
            norm_root(3)

        @block.vector
        def _(dve):
            steps = [0]

            def chain(ins):
                steps[0] += 1
                ins.then_inc(dve_step, 1)
                dve.wait_ge(dve_step, steps[0])

            def split_lo(n):
                dve.wait_ge(h_ready, (n + 1).value())
                dve.tensor_tensor(weight_lo[:, n.at(4), :], raw[:, n.at(4), :], weight_hi[:, n.at(4), :].bitcast(F32),
                                  ALU.subtract).then_inc(l_ready, 1)

            for c in range(8):
                dve.wait_ge(mem_h, c + 1)
                two = slice(2 * c, 2 * c + 2)
                dve.tensor_tensor(mem_lo[:, two, :], mem_raw[:, two, :], mem_hi[:, two, :].bitcast(F32), ALU.subtract)\
                   .then_inc(mem_l, 1)
                if c == 0:
                    split_lo(Nth(0))
            split_lo(Nth(1))
            split_lo(Nth(2))

            def row_stats(t, src):
                for c in range(4):
                    last = dve.bn_stats(stats[:, t, c, :], src[:, t, c * 512:(c + 1) * 512])
                chain(last)
                chain(dve.bn_aggr(mv[:, t, :], stats[:, t, :, :].rearrange("p c k -> p (c k)")))

            def want_root():
                dve.tensor_scalar(rstd, mv[:, :, 1], LN_EPS, None, ALU.add).then_inc(var_ready, 1)

            def norm_rows(k, src, rows, done):
                dve.wait_ge(root_ready, k)
                chain(dve.reciprocal(rstd, rstd))
                for t in range(TT):
                    chain(dve.tensor_scalar(src[:, t, :], src[:, t, :], mv[:, t, 0:1], rstd[:, t:t + 1], ALU.subtract,
                                            ALU.mult))
                    chain(dve.tensor_tensor(src[:, t, :], src[:, t, :], rows[:, 0, :], ALU.mult))
                    dve.tensor_tensor(src[:, t, :], src[:, t, :], rows[:, 1, :], ALU.add).then_inc(done, 1)

            def lo_of_turned(b, k0):
                t, k = b // 4, 4 * (b % 4)
                dve.wait_ge(turned_h, k0 + b + 1)
                dve.tensor_tensor(act_lo[:, k:k + 4, t * P:(t + 1) * P],
                                  side[b % 4][:].rearrange("p (k t) -> p k t", k=4),
                                  act_hi[:, k:k + 4, t * P:(t + 1) * P].bitcast(F32), ALU.subtract)\
                   .then_inc(turned_l, 1)

            def lower_bounds(first):
                if first:
                    dve.wait_ge(const_in, 16 * 8)
                    chain(dve.tensor_tensor(lb_max, lbl[:, :, 0, :], lbl[:, :, 1, :], ALU.max))
                    for layer in range(2):
                        ins = dve.tensor_tensor(lbl[:, :, layer, :], lbl[:, :, layer, :], lb_max, ALU.subtract)
                    ins.then_inc(lb_diff, 1)
                else:
                    dve.wait_ge(lb_exp, 1)
                    chain(dve.tensor_tensor(lb_max, lbl[:, :, 0, :], lbl[:, :, 1, :], ALU.add))
                    chain(dve.reciprocal(lb_max, lb_max))
                    chain(dve.tensor_tensor(lb, lbl[:, :, 0, :], lb_max, ALU.mult))
                    chain(dve.tensor_scalar(lb_rest, lb, -1.0, 1.0, ALU.mult, ALU.add))

            def angles():
                a, turns, r = sin[:], prob[:, 0, :], prob[:, 1, :]
                chain(dve.tensor_copy(a, cos[:].bitcast(I32)))
                chain(dve.tensor_scalar(a, a, invf, None, ALU.mult))
                chain(dve.tensor_scalar(turns, a, float(1 / (2 * np.pi)), ROUND, ALU.mult, ALU.add))
                chain(dve.tensor_scalar(turns, turns, ROUND, None, ALU.subtract))
                chain(dve.scalar_tensor_tensor(out=r, in0=turns, scalar=-PI_A, in1=a, op0=ALU.mult, op1=ALU.add))
                chain(dve.scalar_tensor_tensor(out=a, in0=turns, scalar=-PI_B, in1=r, op0=ALU.mult, op1=ALU.add))
                chain(dve.scalar_tensor_tensor(out=r, in0=turns, scalar=-float(PI_C), in1=a, op0=ALU.mult, op1=ALU.add))
                chain(dve.tensor_scalar(r, r, 3.1415925, -3.1415925, ALU.min, ALU.max))
                chain(dve.scalar_tensor_tensor(out=turns, in0=r, scalar=-1.0, in1=r, op0=ALU.mult, op1=ALU.max))
                dve.tensor_scalar(turns, turns, -1.0, float(np.pi / 2), ALU.mult, ALU.add).then_inc(angle, 1)

            def rotate(x1, x2, r1, r2, t1, t2, c, s):
                chain(dve.tensor_tensor(t1, x1, c, ALU.mult))
                chain(dve.tensor_tensor(t2, x2, s, ALU.mult))
                chain(dve.tensor_tensor(r1, t1, t2, ALU.subtract))
                chain(dve.tensor_tensor(t1, x2, c, ALU.mult))
                chain(dve.tensor_tensor(t2, x1, s, ALU.mult))
                return dve.tensor_tensor(r2, t1, t2, ALU.add)

            def hg_make(p, s):
                if s > 8:
                    return
                hs = slice(2 * p, 2 * p + 2)
                k = 9 * p + s
                if k:
                    dve.wait_ge(hg_packed_q, k)
                    dve.wait_ge(hg_packed_k, k + p - (s == 0))
                if s == 0:
                    if p == 0:
                        for g in (2, 3):
                            wait_taken(dve, GROUP["q_hg"] + g)
                        dve.wait_ge(f_done, 8)
                    dve.tensor_scalar(pre_c[:], f_fw[:, hs, :], -1.0, 1.0, ALU.mult, ALU.add)
                    dve.tensor_scalar(pre_d[:], f_bw[:, hs, :], -1.0, 1.0, ALU.mult, ALU.add)
                    dve.tensor_tensor(pre_a[:], q_hg[:, hs, :], f_fw[:, hs, :], ALU.mult)
                    dve.tensor_tensor(pre_b[:], q_hg[:, hs, :], f_bw[:, hs, :], ALU.mult).then_inc(hg_made, 1)
                    return
                if s == 1:
                    return
                w = 1 << (s - 2)
                n = T // (2 * w)
                dve.wait_ge(hg_made, 8 * p + s - 1)

                def totals(tot, f):
                    if s == 2:
                        return f[:, hs, :].rearrange("p h (b e) -> p (h b) e", e=2)
                    at_ = 2 * T - 4 * T // w
                    flat = tot[:].rearrange("p h t -> p (h t)")
                    return flat[:, at_:at_ + 2 * T // w].rearrange("p (b e) -> p b e", e=2)

                def blocks(a, hand):
                    return a[:].rearrange("p h (b e c) -> p (h b) e c", e=2, c=w)[:, :, hand, :]

                for a, hand, tot, f in ((pre_a, 1, tot_fw, f_fw), (pre_b, 0, tot_bw, f_bw),
                                        (pre_c, 0, tot_fw, f_fw), (pre_d, 1, tot_bw, f_bw)):
                    by = totals(tot, f)[:, :, 1 - hand:2 - hand].to_broadcast([P, 2 * n, w])
                    last = dve.tensor_tensor(blocks(a, hand), blocks(a, hand), by, ALU.mult)
                if s < 8:
                    at_ = 2 * T - 4 * T // (2 * w)
                    for tot, f in ((tot_fw, f_fw), (tot_bw, f_bw)):
                        pairs = totals(tot, f)
                        flat = tot[:].rearrange("p h t -> p (h t)")
                        last = dve.tensor_tensor(flat[:, at_:at_ + 2 * n], pairs[:, :, 0], pairs[:, :, 1], ALU.mult)
                last.then_inc(hg_made, 1)

            def hg_take(p, s):
                if s in (10, 12):
                    return
                k = hg_count(p, s)
                bank = side[k % 2]
                dve.wait_ge(hg_mult, k + 1)
                if k:
                    dve.wait_ge(hg_taken, k)
                blocks = bank[:].rearrange("p (h m t) -> p h m t", h=2, m=2)
                if s == 0:
                    dve.tensor_copy(att[:], blocks).then_inc(hg_taken, 1)
                elif s <= 7:
                    mask = masks[:, s - 1:s, :].to_broadcast([P, 4, P])
                    dve.copy_predicated(att[:].rearrange("p h m t -> p (h m) t"), mask,
                                        bank[:].rearrange("p (b t) -> p b t", b=4)).then_inc(hg_taken, 1)
                elif s == 8:
                    dve.tensor_copy(att_x[:], blocks).then_inc(hg_taken, 1)
                elif s == 9:
                    dve.tensor_copy(q_hg[:, 2 * p:2 * p + 2, :], bank[:].rearrange("p (h t) -> p h t", h=2))\
                       .then_inc(hg_taken, 1)
                else:
                    dve.tensor_scalar(hg_rs[:], bank[:].rearrange("p (h t) -> p h t", h=2), 1.0 / P, RMS_EPS, ALU.mult,
                                      ALU.add).then_inc(hg_taken, 1)

            def hg_norm(p):
                dve.wait_ge(hg_root, p + 1)
                chain(dve.reciprocal(hg_rs[:], hg_rs[:]))
                o = q_hg[:, 2 * p:2 * p + 2, :]
                dve.scalar_tensor_tensor(out=o, in0=o, scalar=hgain, in1=hg_rs[:], op0=ALU.mult, op1=ALU.mult)\
                   .then_inc(hg_normed, 1)

            def attention(n):
                u = unit_at(n, 1)
                if u is not None:
                    dve.wait_ge(scored, u + 1)
                    if u >= 1:
                        dve.wait_ge(exped, u)
                    chain(dve.reduce_max(row_max, side[2][:].rearrange("p (t k) -> p t k", t=2), AX_X))
                    scale = MLA_SCALE if u < HEADS else MEM_SCALE
                    dve.tensor_scalar(row_max, row_max, -scale, None, ALU.mult).then_inc(maxed, 1)
                u = unit_at(n, 2)
                if u is not None:
                    dve.wait_ge(exped, u + 1)
                    chain(dve.reciprocal(row_sum, row_sum))
                    for t in range(TT):
                        last = dve.tensor_scalar(prob[:, t, :], prob[:, t, :], row_sum[:, t:t + 1], None, ALU.mult)
                    last.then_inc(p_done, 1)
                u = unit_at(n, 4)
                if u is not None:
                    dve.wait_ge(y_h, u + 1)
                    if u < HEADS:
                        dve.tensor_tensor(ym_lo[:, u, :], side[3][:, 0:T], ym_hi[:, u, :].bitcast(F32), ALU.subtract)\
                           .then_inc(y_l, 1)
                    else:
                        b = 2 * (u - HEADS)
                        dve.tensor_tensor(yc_lo[:, b:b + 2, :], side[3][:].rearrange("p (k t) -> p k t", k=2),
                                          yc_hi[:, b:b + 2, :].bitcast(F32), ALU.subtract).then_inc(y_l, 1)

            def slot(n):
                if n == 1:
                    for t in range(TT):
                        dve.wait_ge(x_in[t], 16)
                        row_stats(t, h_tok)
                    want_root()
                split_lo(Nth(n + LOOK))
                if n == 2:
                    dve.wait_ge(rows_in, 32)
                    norm_rows(1, h_tok, ln0_rows, h_done)
                if n == 3:
                    lower_bounds(True)
                    angles()
                if n == 5:
                    lower_bounds(False)
                if LN_SLOT < n <= LN_SLOT + 8:
                    lo_of_turned(n - 1 - LN_SLOT, 0)
                for d, (name, f) in enumerate((("f_fw", f_fw), ("f_bw", f_bw))):
                    j = n - FIRST[name]
                    if 2 <= j <= 8 and j % 2 == 0:
                        wait_taken(dve, GROUP[name] + j // 2 - 1)
                        for h in (j - 2, j - 1):
                            last = dve.tensor_scalar(f[:, h, :], f[:, h, :], lb_rest[:, d, h:h + 1], lb[:, d, h:h + 1],
                                                     ALU.mult, ALU.add)
                        last.then_inc(f_done, 1)
                for j in range(2):
                    if n == FIRST["c_q"] + 5 + 4 * j:
                        dve.wait_ge(c_summed, j + 1)
                        dve.tensor_scalar(c_rs[:], side[2][:, 0:T], 1.0 / RANK, RMS_EPS, ALU.mult, ALU.add)\
                           .then_inc(c_var, 1)
                    if n == FIRST["c_q"] + 6 + 4 * j:
                        dve.wait_ge(c_root, j + 1)
                        chain(dve.reciprocal(c_rs[:], c_rs[:]))
                        for b in range(KR * j, KR * (j + 1)):
                            last = dve.scalar_tensor_tensor(out=c_raw[:, b, :], in0=c_raw[:, b, :],
                                                            scalar=cgain[:, b:b + 1], in1=c_rs[:],
                                                            op0=ALU.mult, op1=ALU.mult)
                        last.then_inc(c_scaled, 1)
                        s = slice(KR * j, KR * (j + 1))
                        dve.wait_ge(c_hi_done, j + 1)
                        dve.tensor_tensor(c_lo[:, s, :], c_raw[:, s, :], c_hi[:, s, :].bitcast(F32), ALU.subtract)\
                           .then_inc(c_lo_done, 1)
                if n == FIRST["uq_rope"] + 2:
                    for b in range(2):
                        wait_taken(dve, GROUP["uq_rope"] + b)
                    dve.wait_ge(trig, 2)
                    c, s = (a[:].rearrange("p (o t) -> p o t", o=1).to_broadcast([P, 2, T]) for a in (cos, sin))
                    rotate(rope_x[:, 0], rope_x[:, 1], q_rope[:, 0], q_rope[:, 1], rope_t[:, 0], rope_t[:, 1], c, s)\
                        .then_inc(q_rotated, 1)
                if n == FIRST["k_rope"] + 3:
                    wait_taken(dve, GROUP["k_rope"])
                    rotate(rope_x[:, 0, 0], rope_x[:, 0, 1], rope_t[:, 0, 0], rope_t[:, 0, 1], rope_t[:, 1, 0],
                           rope_t[:, 1, 1], cos[:], sin[:]).then_inc(k_rotated, 1)
                    dve.wait_ge(k_rotated, 1)
                    for h in range(4):
                        last = dve.tensor_scalar(k_rope[:, h, :, :], rope_t[:, 0], head_rows[:, h:h + 1], None, ALU.mult)
                    last.then_inc(kz_done, 1)
                now = hg_at(n, 0)
                if now:
                    hg_make(*now)
                now = hg_at(n, 2)
                if now:
                    hg_take(*now)
                now = hg_at(n, 4)
                if now and now[1] == 11:
                    hg_norm(now[0])
                if n == HG_END + 3:
                    dve.wait_ge(g_open, 1)
                    dve.wait_ge(hg_normed, 4)
                    dve.tensor_tensor(q_hg[:], q_hg[:], g_hg[:], ALU.mult).then_inc(hg_gated, 1)
                if n == HG_END + 5:
                    dve.wait_ge(yh_h, 1)
                    dve.tensor_tensor(yh_lo[:], q_hg[:], yh_hi[:].bitcast(F32), ALU.subtract).then_inc(yh_l, 1)
                attention(n)

            for n in range(1, FIRST["branch"]):
                slot(n)
            n = FIRST["branch"]
            split_lo(Nth(n + LOOK))
            g0 = GROUP["branch"]
            with dve.Fori(0, 2) as i:
                for cg in range(4):
                    acc = merged[:, cg % 2, :].rearrange("p (b t) -> p b t", b=2)
                    for b in range(3):
                        j = 3 * cg + b
                        split_lo(Nth(n + 1 + LOOK + j, i, 12))
                        dve.wait_ge(piece_used, (Nth(n + 1 + j, i, 12)).value())
                        if b == 0:
                            dve.wait_ge(gates_open, i * 4 + (cg + 1))
                        src = pair[(g0 + j) % 2][:, :, 0:T]
                        by = gate[:, cg % 2, b, :].rearrange("p (b t) -> p b t", b=2)
                        group = Nth(g0 + j, i, 12)
                        free = pair_free[group.at(2)]
                        if b == 0:
                            dve.tensor_tensor(acc, src, by, ALU.mult).then_inc(free, 1)
                            wait_taken(dve, group)
                        else:
                            prod = product[:].rearrange("p (b t) -> p b t", b=2)
                            dve.tensor_tensor(prod, src, by, ALU.mult).then_inc(free, 1)
                            wait_taken(dve, group)
                            if b == 1:
                                dve.tensor_tensor(acc, acc, prod, ALU.add).then_inc(merge_part, 1)
                                dve.wait_ge(merge_part, i * 4 + (cg + 1))
                            else:
                                dve.tensor_tensor(acc, acc, prod, ALU.add).then_inc(merged_sum, 1)
                                dve.wait_ge(merged_h, i * 4 + (cg + 1))
                                dst = bass.ds(i * 8 + 2 * cg, 2)
                                dve.tensor_tensor(act_lo[:, dst, :], acc, act_hi[:, dst, :].bitcast(F32), ALU.subtract)\
                                   .then_inc(merged_l, 1)
            n = FIRST["w_o"]
            g0 = GROUP["w_o"]

            def residual(g, c):
                zc = z[:, :, c * 512:(c + 1) * 512]
                dve.scalar_tensor_tensor(out=zc, in0=zc, scalar=ALPHA, in1=pair[g % 2][:], op0=ALU.mult, op1=ALU.add)\
                   .then_inc(pair_free[g % 2], 1)
                wait_taken(dve, g)
                for t in range(TT):
                    last = dve.bn_stats(stats[:, t, c, :], z[:, t, c * 512:(c + 1) * 512])
                return last

            def want_root_of_sums(last):
                chain(last)
                for t in range(TT):
                    ins = dve.bn_aggr(mv[:, t, :], stats[:, t, :, :].rearrange("p c k -> p (c k)"))
                chain(ins)
                want_root()

            for c in range(4):
                for j in range(4):
                    split_lo(Nth(n + 1 + LOOK + 4 * c + j))
                if c == 0:
                    dve.wait_ge(z_in, 16)
                dve.wait_ge(piece_used, n + 4 * c + 4)
                last = residual(g0 + c, c)
            want_root_of_sums(last)
            dve.wait_ge(rows1_in, 32)
            norm_rows(2, z, ln1_rows, h_done)
            for b in range(8):
                lo_of_turned(b, 8)
            n = FIRST["ffn"]
            g0 = GROUP["ffn"]
            with dve.Fori(0, 22) as i:
                for j in range(4):
                    split_lo(Nth(n + 1 + LOOK + j, i, 4))
                    if j == 3:
                        dve.wait_ge(piece_used, Nth(n + 4, i, 4).value())
                        wait_taken(dve, Nth(g0, i, 2))
                        dve.tensor_tensor(ff[:].rearrange("p (b t) -> p b t", b=2), pair[(g0 + 1) % 2][:, :, 0:T],
                                          silu[:].rearrange("p (b t) -> p b t", b=2), ALU.mult).then_inc(pair_free[(g0 + 1) % 2], 1)
                        dve.wait_ge(ff_h, i + 1)
                        dst = bass.ds(i * 2, 2)
                        dve.tensor_tensor(ff_lo[:, dst, :], ff[:].rearrange("p (b t) -> p b t", b=2),
                                          ff_hi[:, dst, :].bitcast(F32), ALU.subtract).then_inc(ff_l, 1)
            n = FIRST["down"]
            g0 = GROUP["down"]
            for m in range(n + 1, PIECES + 1):
                if m + LOOK < PIECES:
                    split_lo(Nth(m + LOOK))
                if (m - n) % 11 == 0:
                    c = (m - n) // 11 - 1
                    dve.wait_ge(piece_used, m)
                    last = residual(g0 + c, c)
            want_root_of_sums(last)
            dve.wait_ge(rows2_in, 32)
            norm_rows(3, z, ln2_rows, out_rows)

        @block.tensor
        def _(pe):
            def begin(n):
                pe.wait_ge(l_ready, n.value() + 1)

            def begin_group(g):
                g = g if isinstance(g, Nth) else Nth(g)
                if g.c >= 2:
                    wait_taken(pe, g + -2)

            def features(n, out, width, column, kts, k0, hi, lo, first, last):
                w_hi = weight_hi[:, n.at(4), :].rearrange("p (k c) -> p k c", c=width)
                w_lo = weight_lo[:, n.at(4), :].rearrange("p (k c) -> p k c", c=width)
                for k in range(kts):
                    f = slice(column, column + P)
                    a = k0 + k
                    pe.matmul(out, w_hi[:, k, f], hi[:, a, :], start=first and k == 0, stop=False)
                    pe.matmul(out, w_hi[:, k, f], lo[:, a, :], start=False, stop=False)
                    mm = pe.matmul(out, w_lo[:, k, f], hi[:, a, :], start=False, stop=last and k == kts - 1)
                return mm

            def tokens(n, g, k0, hi, lo, first, last):
                w_hi = weight_hi[:, n.at(4), :].rearrange("p (k c) -> p k c", c=512)
                w_lo = weight_lo[:, n.at(4), :].rearrange("p (k c) -> p k c", c=512)
                begin(n)
                for t in range(TT):
                    out = pair[g % 2][:, t, :]
                    for k in range(4):
                        tok = slice(t * P, (t + 1) * P)
                        pe.matmul(out, hi[:, k0 + k, tok], w_hi[:, k, :], start=first and k == 0, stop=False)
                        pe.matmul(out, hi[:, k0 + k, tok], w_lo[:, k, :], start=False, stop=False)
                        mm = pe.matmul(out, lo[:, k0 + k, tok], w_hi[:, k, :], start=False, stop=last and k == 3)
                mm.then_inc(piece_used, 1)

            def f_piece(n, g, half, hi, lo, halves=2):
                begin(n)
                if half == 0:
                    begin_group(g)
                for b in range(2):
                    mm = features(n, pair[g.at(2)][:, b, 0:T], 256, b * P, 8, 8 * half, hi, lo, half == 0,
                                  half == halves - 1)
                mm.then_inc(piece_used, 1)

            def t_piece(n, g, quarter, quarters, hi, lo):
                if quarter == 0:
                    begin_group(g)
                tokens(n, g, 4 * quarter, hi, lo, quarter == 0, quarter == quarters - 1)

            def four_blocks(n, g, hi, lo, k0):
                begin(n)
                for b in range(4):
                    if b % 2 == 0:
                        begin_group(g + b // 2)
                    mm = features(n, pair[(g + b // 2) % 2][:, b % 2, 0:T], 512, b * P, 4, k0, hi, lo, True, True)
                mm.then_inc(piece_used, 1)

            def turn(b, src, k0, rows):
                t, k = b // 4, 4 * (b % 4)
                pe.wait_ge(rows, (2 if k0 else 0) + t + 1)
                if b >= 4:
                    pe.wait_ge(turned_l, k0 + b - 3)
                for j in range(4):
                    mm = pe.transpose(side[b % 4][:, j * P:(j + 1) * P], src[:, t, (k + j) * P:(k + j + 1) * P], ident[:])
                mm.then_inc(turned, 1)

            def hg_multiply(p, s):
                if s in (10, 12):
                    return
                k = hg_count(p, s)
                bank = side[k % 2]
                if k >= 2:
                    pe.wait_ge(hg_taken, k - 1)
                if s <= 8:
                    pe.wait_ge(hg_packed_q, 9 * p + s + 1)
                    pe.wait_ge(hg_packed_k, 10 * p + s + 1)
                    for h in range(2):
                        for m in range(TT):
                            keys = m if s < 8 else 1 - m
                            mm = pe.matmul(bank[:, (2 * h + m) * P:(2 * h + m + 1) * P],
                                           k_hat[:, k % 2, h, keys * P:(keys + 1) * P],
                                           q_hat[:, k % 2, h, m * P:(m + 1) * P], start=True, stop=True)
                elif s == 9:
                    pe.wait_ge(hg_taken, k)
                    for h in range(2):
                        for m in range(TT):
                            o = bank[:, (2 * h + m) * P:(2 * h + m + 1) * P]
                            v = slice((2 * p + h) * VD, (2 * p + h + 1) * VD)
                            pe.matmul(o, v_hg[:, m, v], att[:, h, m, :], start=True, stop=False)
                            mm = pe.matmul(o, v_hg[:, 1 - m, v], att_x[:, h, m, :], start=False, stop=True)
                else:
                    pe.wait_ge(hg_packed_k, 10 * (p + 1))
                    mm = pe.matmul(bank[:], ones[:], k_hat[:, k % 2].rearrange("p h t -> p (h t)"), start=True,
                                   stop=True)
                mm.then_inc(hg_mult, 1)

            def attention(n):
                u = unit_at(n, 2)
                if u is not None:
                    pe.wait_ge(p_done, u + 1)
                    if u >= 1:
                        pe.wait_ge(y_l, u)
                    for k in range(2):
                        for t in range(TT):
                            at_ = k * T + t * P
                            mm = pe.transpose(side[3][:, at_:at_ + P], prob[:, t, k * P:(k + 1) * P], ident[:])
                    mm.then_inc(p_turned, 1)
                u = unit_at(n, 3)
                if u is not None:
                    pe.wait_ge(pt_done, u + 1)
                    if u < HEADS:
                        for k in range(2):
                            mm = pe.matmul(side[3][:, 0:T], v_mla[:, k, u * VD:(u + 1) * VD], prob_t[:, k, :],
                                           start=k == 0, stop=k == 1)
                    else:
                        for b in range(2):
                            f = (2 * (u - HEADS) + b) * P
                            for k in range(2):
                                mm = pe.matmul(side[3][:, b * T:(b + 1) * T],
                                               v_mem[:, f // 512, k, f % 512:f % 512 + P], prob_t[:, k, :],
                                               start=k == 0, stop=k == 1)
                    mm.then_inc(valued, 1)
                u = unit_at(n, 0)
                if u is not None:
                    if u == 0:
                        pe.wait_ge(kz_done, 1)
                        pe.wait_ge(c_var, 2)
                    else:
                        pe.wait_ge(exped, u)
                    if u == HEADS:
                        pe.wait_ge(mem_back, 48)
                    for t in range(TT):
                        out, tok = side[2][:, t * T:(t + 1) * T], slice(t * P, (t + 1) * P)
                        if u < HEADS:
                            pe.matmul(out, q_nope[:, u, tok], k_nope[:, u, :], start=True, stop=False)
                            for r in range(2):
                                mm = pe.matmul(out, q_rope[:, r, u // 4, tok], k_rope[:, u % 4, r, :], start=False,
                                               stop=r == 1)
                        else:
                            for j in range(2):
                                b = 2 * (u - HEADS) + j
                                mm = pe.matmul(out, q_mem[:, b, tok], k_mem[:, b, :], start=j == 0, stop=j == 1)
                    mm.then_inc(scored, 1)

            def after(n):
                if LN_SLOT <= n < LN_SLOT + 8:
                    turn(n - LN_SLOT, h_tok, 0, h_done)
                for j in range(2):
                    if n == FIRST["c_q"] + 4 + 4 * j:
                        pe.wait_ge(c_squared, j + 1)
                        if j:
                            pe.wait_ge(c_var, j)
                        for b in range(KR):
                            mm = pe.matmul(side[2][:, 0:T], ones[:], c_sq[:, b, :], start=b == 0, stop=b == KR - 1)
                        mm.then_inc(c_summed, 1)
                now = hg_at(n, 1)
                if now:
                    hg_multiply(*now)
                attention(n)

            def f_phase(name, count, hi, lo):
                for j in range(count):
                    n = FIRST[name] + j
                    if name == "mem_k":
                        pe.wait_ge(mem_l, 4 * (j % 2) + 4)
                    f_piece(Nth(n), Nth(GROUP[name] + j // 2), j % 2, hi, lo)
                    after(n)

            def t_phase(name, count, quarters, hi, lo):
                for j in range(count):
                    n = FIRST[name] + j
                    if name == "w_o" and j < quarters:
                        pe.wait_ge(merged_l, 2 * j + 2)
                    if name == "down" and j < quarters:
                        pe.wait_ge(ff_l, 2 * j + 2)
                    t_piece(Nth(n), GROUP[name] + j // quarters, j % quarters, quarters, hi, lo)
                    after(n)

            pe.wait_ge(const_in, 16 * 8)
            pe.wait_ge(ones_set, 1)
            f_phase("mem_k", 8, mem_hi, mem_lo)
            t_phase("mem_v", 8, 4, mem_hi, mem_lo)
            pe.wait_ge(turned_l, 8)
            f_phase("c_q", 4, act_hi, act_lo)
            f_phase("c_kv", 4, act_hi, act_lo)
            f_piece(Nth(FIRST["f_fw"]), Nth(GROUP["f_fw"]), 0, act_hi, act_lo)
            after(FIRST["f_fw"])
            f_piece(Nth(FIRST["f_fw"] + 1), Nth(GROUP["f_fw"]), 1, act_hi, act_lo)
            f_piece(Nth(FIRST["f_fw"] + 2), Nth(GROUP["f_fw"] + 1), 0, act_hi, act_lo)
            f_piece(Nth(FIRST["f_fw"] + 3), Nth(GROUP["f_fw"] + 1), 1, act_hi, act_lo)
            with pe.Fori(0, 5) as i:
                for j in range(4):
                    f_piece(Nth(FIRST["f_fw"] + 4 + j, i, 4), Nth(GROUP["f_fw"] + 2 + j // 2, i, 2), j % 2, act_hi,
                            act_lo)
            t_phase("i_hg", 8, 4, act_hi, act_lo)
            for name, c in (("uq_nope", 0), ("uq_rope", 0), ("uk", 1)):
                pe.wait_ge(c_lo_done, c + 1)
                for j in range(GROUPS[name] // 2):
                    n = FIRST[name] + j
                    four_blocks(Nth(n), GROUP[name] + 2 * j, c_hi, c_lo, KR * c)
                    after(n)
            for j in range(2):
                n = FIRST["uv"] + j
                begin_group(GROUP["uv"] + j)
                tokens(Nth(n), GROUP["uv"] + j, KR, c_hi, c_lo, True, True)
                after(n)
            begin_group(GROUP["k_rope"])
            for r in range(2):
                n = Nth(FIRST["k_rope"] + r)
                begin(n)
                features(n, pair[GROUP["k_rope"] % 2][:, r, 0:T], P, 0, KD, 0, act_hi, act_lo, True, True)\
                    .then_inc(piece_used, 1)
                after(n.c)
            f_phase("q_mem", 8, act_hi, act_lo)
            f_phase("g_hg", 8, act_hi, act_lo)
            f_phase("gates", 48, act_hi, act_lo)
            pe.wait_ge(yh_l, 1)
            pe.wait_ge(y_l, UNITS_ATTN)
            with pe.Fori(0, 2) as i:
                for j in range(12):
                    hi, lo = ((yh_hi, yh_lo), (ym_hi, ym_lo), (yc_hi, yc_lo))[j % 3]
                    f_piece(Nth(FIRST["branch"] + j, i, 12), Nth(GROUP["branch"] + j, i, 12), 0, hi, lo, 1)
            t_phase("w_o", 16, 4, act_hi, act_lo)
            for b in range(8):
                turn(b, z, 8, h_done)
            pe.wait_ge(turned_l, 16)
            with pe.Fori(0, 22) as i:
                for j in range(4):
                    f_piece(Nth(FIRST["ffn"] + j, i, 4), Nth(GROUP["ffn"] + j // 2, i, 2), j % 2, act_hi, act_lo)
            t_phase("down", 44, 11, ff_hi, ff_lo)


def _pieces(inputs):
    w_in, w_uq, w_ukv = inputs["w_in"][0], inputs["mla_w_uq"][0], inputs["mla_w_ukv"][0]
    w_mem, w_branch, w_o = inputs["mem_w_kv"][0], inputs["w_branch"][0], inputs["w_o"][0]
    w_gate, w_up, w_down = inputs["w_ffn_gate"][0], inputs["w_ffn_up"][0], inputs["w_ffn_down"][0]
    at, begin = 0, {}
    for name, width in (("q", BW), ("i", BW), ("f_fw", BW), ("f_bw", BW), ("g", BW), ("c_q", RANK), ("c_kv", RANK),
                        ("k_rope", ROPE), ("q_mem", BW), ("gates", 3 * D)):
        begin[name] = at
        at += width

    def cut(w, k0, kts, columns):
        part = w[k0 * P:(k0 + kts) * P]
        part = part[:, columns]
        return part.reshape(kts, P, -1).transpose(1, 0, 2).reshape(P, PIECE)

    def features(w, c0, width):
        for c in range(c0, c0 + width, 256):
            for half in range(2):
                yield cut(w, 8 * half, 8, slice(c, c + 256))

    def tokens(w, c0, width, quarters=4):
        for c in range(c0, c0 + width, 512):
            for q in range(quarters):
                yield cut(w, 4 * q, 4, slice(c, c + 512))

    heads = np.arange(HEADS)
    uq = heads[:, None] * (NOPE + ROPE)
    nope = uq + np.arange(NOPE)
    rope = uq + NOPE + np.arange(HALF)
    ukv = heads[:, None] * (NOPE + VD)
    yield from features(w_mem, 0, BW)
    yield from tokens(w_mem, BW, BW)
    yield from features(w_in, begin["c_q"], RANK)
    yield from features(w_in, begin["c_kv"], RANK)
    for name in ("f_fw", "f_bw", "q"):
        yield from features(w_in, begin[name], BW)
    yield from tokens(w_in, begin["i"], BW)
    for four in range(2):
        yield cut(w_uq, 0, KR, nope[4 * four:4 * four + 4].ravel())
    yield cut(w_uq, 0, KR, np.concatenate([rope.ravel(), (rope + HALF).ravel()]))
    for part in (0, NOPE):
        for four in range(2):
            yield cut(w_ukv, 0, KR, (ukv + part + np.arange(P))[4 * four:4 * four + 4].ravel())
    for r in range(2):
        yield cut(w_in, 0, KD, np.tile(begin["k_rope"] + r * HALF + np.arange(HALF), 4))
    yield from features(w_in, begin["q_mem"], BW)
    yield from features(w_in, begin["g"], BW)
    for c in range(0, D, 256):
        for b in range(3):
            yield from features(w_in, begin["gates"] + b * D + c, 256)
    for c in range(0, D, 256):
        for b in range(3):
            yield cut(w_branch[b], 0, 8, slice(c, c + 256))
    yield from tokens(w_o, 0, D)
    for c in range(0, DFF, 256):
        yield from features(w_gate, c, 256)
        yield from features(w_up, c, 256)
    yield from tokens(w_down, 0, D, KF // 4)


def kernel(**inputs):
    import concourse.bacc as bacc
    from concourse.bass_utils import run_bass_kernel_spmd

    inputs = {name: np.asarray(a) for name, a in inputs.items()}
    stream = np.empty((PIECES, P, PIECE), np.float32)
    n = 0
    for n, piece in enumerate(_pieces(inputs)):
        stream[n] = piece
    assert n == PIECES - 1

    def per_partition(a):
        return np.ascontiguousarray(np.moveaxis(a.reshape(a.shape[:-1] + (-1, P)), -1, 0).reshape(P, -1))

    bits = np.arange(P)[:, None] ^ np.arange(P)[None, :]
    masks = np.stack([(bits >> level) == 1 for level in range(LEVELS - 1)], axis=1).astype(np.int32)
    arrays = {
        "stream": stream,
        "mem_t": np.ascontiguousarray(inputs["mem"][0].T.reshape(KD, P, T).transpose(1, 0, 2)),
        "x": np.ascontiguousarray(inputs["x"][0]),
        "pos": np.ascontiguousarray(inputs["positions"]),
        "ln_rows": np.stack([inputs["ln_emb_g"], inputs["ln_emb_b"], inputs["ln1_g"][0], inputs["ln1_b"][0],
                             inputs["ln2_g"][0], inputs["ln2_b"][0]]),
        "lb_logits": per_partition(inputs["hgrn_lb_logits"]),
        "hg_gain": np.ascontiguousarray(inputs["hgrn_norm_g"][0][:, None]),
        "c_gains": per_partition(np.stack([inputs["mla_g_cq"][0], inputs["mla_g_ckv"][0]])),
        "inv_freq": np.tile((np.float32(ROPE_THETA) ** (-np.arange(HALF, dtype=np.float32) / np.float32(HALF)))
                            .astype(np.float32), 4)[:, None],
        "identity": np.eye(P, dtype=np.float32),
        "level_masks": masks,
        "head_mask": np.repeat(np.eye(4, dtype=np.float32), HALF, axis=0),
    }
    nc = bacc.Bacc("TRN2", target_bir_lowering=False, num_devices=1, dynamic_dma_scratch_size=1024)
    args = [nc.dram_tensor(f"in_{name}", a.shape, mybir.dt.from_np(a.dtype), kind="ExternalInput").ap()
            for name, a in arrays.items()]
    out = nc.dram_tensor("out", (T, D), F32, kind="ExternalOutput").ap()
    encoder_program(nc, *args, out)
    r = run_bass_kernel_spmd(nc, [{f"in_{name}": a for name, a in arrays.items()}], core_ids=[0])
    return r.results[0]["out"].reshape(1, T, D)
```

```python
from contextlib import ExitStack

import numpy as np
import concourse.bass as bass
from concourse import mybir

F32 = mybir.dt.float32
F32R = mybir.dt.float32r
I32 = mybir.dt.int32
ALU = mybir.AluOpType
ACT = mybir.ActivationFunctionType

P = 128
D = 2048
T = 256
TT = T // P
KD = D // P
BW = 1024
NB = BW // P
RANK = 512
KR = RANK // P
HEADS = 8
NOPE, ROPE, VD = 128, 64, 128
HALF = ROPE // 2
MEM_HEADS, MEM_HD = 4, 256
DFF = 5632
KF = DFF // P
PIECE = 2048
ALPHA = 2.0 ** 0.25
LN_EPS, RMS_EPS = 1e-5, 1e-6
MLA_SCALE = float(NOPE + ROPE) ** -0.5
MEM_SCALE = float(MEM_HD) ** -0.5
ROPE_THETA = 10000.0
LEVELS = 8
PI_A, PI_B = 6.28125, 0.0019350051879882812
PI_C = 2 * np.pi - PI_A - PI_B
ROUND = 12582912.0

PHASES = [("mem_k", 8), ("mem_v", 8), ("c_q", 4), ("c_kv", 4), ("f_fw", 8), ("f_bw", 8), ("q_hg", 8), ("i_hg", 8),
          ("uq_nope", 2), ("uq_rope", 1), ("uk", 2), ("uv", 2), ("k_rope", 1), ("q_mem", 8), ("g_hg", 8),
          ("gates", 48), ("branch", 24), ("w_o", 16), ("ffn", 88), ("down", 44)]
FIRST = {}
PIECES = 0
for _name, _count in PHASES:
    FIRST[_name] = PIECES
    PIECES += _count
GROUPS = {"mem_k": 4, "mem_v": 2, "q_mem": 4, "g_hg": 4, "f_fw": 4, "f_bw": 4, "q_hg": 4, "i_hg": 2, "c_q": 2, "c_kv": 2,
          "uq_nope": 4, "uq_rope": 2, "uk": 4, "uv": 2, "k_rope": 1, "gates": 24, "branch": 24, "w_o": 4, "ffn": 44,
          "down": 4}
GROUP = {}
_g = 0
for _name, _count in PHASES:
    GROUP[_name] = _g
    _g += GROUPS[_name]

U_KM, U_VM, U_QM, U_G, U_GATES = 0, 4, 8, 12, 16
LOOK = 2
UNITS = U_GATES + 24

STATS_SLOT, NORM_SLOT = 6, 8
CONST_SLOT = 16
LN_SLOT = 11
HG_SLOT, HG_STEPS, PAIRS = FIRST["i_hg"] + 1, 13, 4
HG_END = HG_SLOT + HG_STEPS * PAIRS + 3
ATTN_SLOTS = [FIRST["q_mem"] + 4 + 4 * u for u in range(HEADS)] + [HG_END + 10 + 3 * u for u in range(MEM_HEADS)]
assert ATTN_SLOTS[-1] + 4 < FIRST["branch"]
UNITS_ATTN = len(ATTN_SLOTS)


class Nth:

    def __init__(self, c, i=None, step=0):
        self.c, self.i, self.step = c, i, step

    def __add__(self, k):
        return Nth(self.c + k, self.i, self.step)

    def at(self, m):
        assert self.step % m == 0
        return self.c % m

    def over(self, m):
        assert self.step % m == 0
        return self.c // m if self.i is None else self.i * (self.step // m) + self.c // m

    def value(self):
        return self.over(1)


def hg_count(pair, step):
    return 11 * pair + (step if step < 10 else 10)


def encoder_program(nc, stream, mem_t, x, pos, ln_rows, lb_logits, hg_gain, c_gains, inv_freq, identity, level_masks,
                    head_mask, out):
    scratch = nc.dram_tensor("scratch", (UNITS, P, 512), F32, kind="Internal").ap()
    h_scratch = nc.dram_tensor("h_scratch", (T, D), F32, kind="Internal").ap()

    KB = 1024
    base = -(-nc.sbuf_base // 128) * 128

    def at(name, kb, shape, dt=F32):
        return nc.alloc_sbuf_tensor_at(name, [P] + shape, dt, offset=base + int(kb * KB))

    raw = at("raw", 0, [4, PIECE])
    weight_lo = at("weight_lo", 0, [4, PIECE], F32R)
    weight_hi = at("weight_hi", 32, [4, PIECE], F32R)
    act_hi = at("act_hi", 64, [KD, T], F32R)
    act_lo = at("act_lo", 80, [KD, T], F32R)
    ln2_rows = at("ln2_rows", 64, [2, D])
    ident = at("ident", 96, [P])
    masks = at("masks", 96.5, [7, P], I32)
    ones = at("ones", 100, [P])
    cos = at("cos", 100.5, [T])
    sin = at("sin", 101.5, [T])
    prob_t = at("prob_t", 100.5, [2, T])
    small = at("small", 102.5, [256])
    f_fw = at("f_fw", 104, [HEADS, T])
    f_bw = at("f_bw", 112, [HEADS, T])
    q_hg = at("q_hg", 120, [HEADS, T])
    v_hg = at("v_hg", 128, [TT, BW])
    pre_a = at("pre_a", 136, [2, T])
    pre_b = at("pre_b", 138, [2, T])
    pre_c = at("pre_c", 140, [2, T])
    pre_d = at("pre_d", 142, [2, T])
    q_hat = at("q_hat", 144, [2, 2, T])
    k_hat = at("k_hat", 148, [2, 2, T])
    att = at("att", 152, [2, 2, P])
    att_x = at("att_x", 154, [2, 2, P])
    hg_rs = at("hg_rs", 154, [2, T])
    tot_fw = at("tot_fw", 156, [2, T])
    tot_bw = at("tot_bw", 158, [2, T])
    yh_hi = at("yh_hi", 104, [NB, T], F32R)
    yh_lo = at("yh_lo", 112, [NB, T], F32R)
    g_hg = at("g_hg", 128, [HEADS, T])
    q_mem = at("q_mem", 120, [NB, T])
    k_mem = at("k_mem", 128, [NB, T])
    v_mem = at("v_mem", 136, [2, TT, 512])
    q_nope = at("q_nope", 160, [HEADS, T])
    q_rope = at("q_rope", 168, [4, T])
    k_nope = at("k_nope", 172, [HEADS, T])
    c_raw = at("c_raw", 180, [2 * KR, T])
    k_rope = at("k_rope", 180, [2, T])
    v_mla = at("v_mla", 188, [TT, BW])
    c_hi = at("c_hi", 196, [2 * KR, T], F32R)
    c_lo = at("c_lo", 204, [2 * KR, T], F32R)
    ym_hi = at("ym_hi", 196, [NB, T], F32R)
    ym_lo = at("ym_lo", 204, [NB, T], F32R)
    yc_hi = at("yc_hi", 160, [NB, T], F32R)
    yc_lo = at("yc_lo", 168, [NB, T], F32R)
    spill = at("spill", 212, [4, 512])
    c_sq = at("c_sq", 136, [KR, T])
    c_rs = at("c_rs", 140, [T])
    rope_x = at("rope_x", 212, [4, T])
    rope_swapped = at("rope_swapped", 216, [4, T])
    prob = at("prob", 220, [2, T])
    mem_raw = at("mem_raw", 164, [KD, T])
    mem_hi = at("mem_hi", 180, [KD, T], F32R)
    mem_lo = at("mem_lo", 196, [KD, T], F32R)
    h_tok = at("h_tok", 104, [TT, D])
    ln0_rows = at("ln0_rows", 120, [2, D])
    gate = at("gate", 176, [2, 3, 512])
    merged = at("merged", 188, [2, 512])
    product = at("product", 192, [512])
    z = at("z", 196, [TT, D])
    ln1_rows = at("ln1_rows", 104, [2, D])
    ff_hi = at("ff_hi", 104, [KF, T], F32R)
    ff_lo = at("ff_lo", 148, [KF, T], F32R)
    silu = at("silu", 192, [512])
    ff = at("ff", 194, [512])

    def cols(a, b):
        return small[:, a:b]

    lbl = small[:, 0:32].rearrange("p (d l h) -> p d l h", d=2, l=2)
    lb = small[:, 32:48].rearrange("p (d h) -> p d h", d=2)
    lb_rest = small[:, 48:64].rearrange("p (d h) -> p d h", d=2)
    lb_max = small[:, 64:80].rearrange("p (d h) -> p d h", d=2)
    hgain = cols(80, 81)
    invf = cols(81, 82)
    cgain = cols(84, 84 + 2 * KR)
    rope_sign = cols(92, 93)
    head_rows = cols(93, 95)
    mv = small[:, 96:100].rearrange("p (t k) -> p t k", t=2)
    rstd = cols(100, 102)
    row_max = cols(104, 106)
    row_sum = cols(106, 108)
    spare = cols(108, 109)
    stats = small[:, 128:176].rearrange("p (t c k) -> p t c k", t=2, c=4)

    with ExitStack() as ctx:
        pair = [ctx.enter_context(nc.psum_tensor(f"pair{i}", [P, 2, 512], F32)) for i in range(2)]
        side = [ctx.enter_context(nc.psum_tensor(f"side{i}", [P, 512], F32)) for i in range(4)]

        def sem(name):
            return ctx.enter_context(nc.semaphore(name))

        raw_full = [sem(f"raw_full{i}") for i in range(4)]
        h_ready = sem("h_ready")
        l_ready = sem("l_ready")
        piece_used = sem("piece_used")
        pair_free = [sem(f"pair_free{i}") for i in range(2)]
        act_step = sem("act_step")
        dve_step = sem("dve_step")
        spilled = [sem(f"spilled{i}") for i in range(4)]
        mem_in = [sem(f"mem_in{i}") for i in range(8)]
        x_in = [sem(f"x_in{i}") for i in range(2)]
        rows_in = sem("rows_in")
        const_in = sem("const_in")
        ident_in = sem("ident_in")
        ones_set = sem("ones_set")
        mem_h = sem("mem_h")
        mem_l = sem("mem_l")
        var_ready = sem("var_ready")
        root_ready = sem("root_ready")
        h_done = sem("h_done")
        h_saved = sem("h_saved")
        turned = sem("turned")
        turned_h = sem("turned_h")
        turned_l = sem("turned_l")
        f_done = sem("f_done")
        lb_diff = sem("lb_diff")
        lb_exp = sem("lb_exp")
        angle = sem("angle")
        trig = sem("trig")
        c_squared = sem("c_squared")
        c_summed = sem("c_summed")
        c_var = sem("c_var")
        c_root = sem("c_root")
        c_scaled = sem("c_scaled")
        c_hi_done = sem("c_hi_done")
        c_lo_done = sem("c_lo_done")
        q_rotated = sem("q_rotated")
        swapped = sem("swapped")
        rope_turned = sem("rope_turned")
        k_rotated = sem("k_rotated")
        kz_done = sem("kz_done")
        hg_made = sem("hg_made")
        hg_packed_q = sem("hg_packed_q")
        hg_packed_k = sem("hg_packed_k")
        hg_mult = sem("hg_mult")
        hg_taken = sem("hg_taken")
        hg_root = sem("hg_root")
        hg_normed = sem("hg_normed")
        hg_gated = sem("hg_gated")
        yh_h = sem("yh_h")
        yh_l = sem("yh_l")
        g_back = sem("g_back")
        g_open = sem("g_open")
        gates_open = sem("gates_open")
        mem_back = sem("mem_back")
        scored = sem("scored")
        maxed = sem("maxed")
        exped = sem("exped")
        p_done = sem("p_done")
        p_turned = sem("p_turned")
        pt_done = sem("pt_done")
        valued = sem("valued")
        y_h = sem("y_h")
        y_l = sem("y_l")
        gate_full = [sem(f"gate_full{i}") for i in range(2)]
        merged_sum = sem("merged_sum")
        merged_h = sem("merged_h")
        merged_l = sem("merged_l")
        z_in = [sem(f"z_in{i}") for i in range(4)]
        rows1_in = sem("rows1_in")
        rows2_in = sem("rows2_in")
        ff_h = sem("ff_h")
        ff_l = sem("ff_l")
        tile_summed = sem("tile_summed")
        out_rows = sem("out_rows")
        merge_part = sem("merge_part")
        out_done = sem("out_done")
        block = ctx.enter_context(nc.Block())

        def turn_bank(b, k0):
            if k0 and b >= 6:
                return side[b - 6][:]
            if k0 and b >= 4:
                return pair[(GROUP["w_o"] + 3) % 2][:, b - 4, :]
            return side[b % 4][:]

        def unit_at(n, later):
            return ATTN_SLOTS.index(n - later) if n - later in ATTN_SLOTS else None

        def wait_taken(eng, g):
            g = g if isinstance(g, Nth) else Nth(g)
            eng.wait_ge(pair_free[g.at(2)], g.over(2) + 1)

        def hg_at(n, later):
            k = n - later - HG_SLOT
            return divmod(k, HG_STEPS) if 0 <= k < HG_STEPS * PAIRS else None

        @block.sync
        def _(sp):
            def load(n):
                if n.c >= 4:
                    sp.wait_ge(piece_used, (n + -3).value())
                src = stream[n.c] if n.i is None else stream[bass.ds(n.value(), 1)].rearrange("o p c -> p (o c)")
                sp.dma_start(raw[:, n.at(4), :], src).then_inc(raw_full[n.at(4)], 16)

            def loads(a, b):
                rounds = (b - a) // 4
                if rounds > 1:
                    with sp.Fori(0, rounds) as i:
                        for j in range(4):
                            load(Nth(a + j, i, 4))
                    a += 4 * rounds
                for n in range(a, b):
                    load(Nth(n))

            def gain_and_bias(dst, row, r, done):
                sp.dma_start(dst[:, r, :], ln_rows[row + r:row + r + 1, :].to_broadcast([P, D])).then_inc(done, 16)

            for c in range(8):
                two = slice(2 * c, 2 * c + 2)
                sp.dma_start(mem_raw[:, two, :], mem_t[:, two, :]).then_inc(mem_in[c], 16)
                if c == 0:
                    load(Nth(0))
                if c == 3:
                    load(Nth(1))
            loads(2, 5)
            for t in range(TT):
                sp.dma_start(h_tok[:, t, :], x[t * P:(t + 1) * P, :]).then_inc(x_in[t], 16)
                load(Nth(5 + t))
            load(Nth(7))
            for r in range(2):
                gain_and_bias(ln0_rows, 0, r, rows_in)
                load(Nth(8 + r))
            sp.dma_start(ident[:], identity).then_inc(ident_in, 16)
            loads(10, 12)
            sp.dma_start(masks[:], level_masks).then_inc(const_in, 16)
            sp.dma_start(small[:, 0:32], lb_logits).then_inc(const_in, 16)
            sp.dma_start(hgain, hg_gain).then_inc(const_in, 16)
            sp.dma_start(invf, inv_freq).then_inc(const_in, 16)
            sp.dma_start(cgain, c_gains).then_inc(const_in, 16)
            sp.dma_start(cols(92, 95), head_mask).then_inc(const_in, 16)
            sp.dma_start(cos[:].bitcast(I32), pos.to_broadcast([P, T])).then_inc(const_in, 16)
            loads(12, 20)
            sp.wait_ge(h_done, 8)
            for t in range(TT):
                sp.dma_start(h_scratch[t * P:(t + 1) * P, :], h_tok[:, t, :]).then_inc(h_saved, 16)
            loads(20, HG_END + 1)
            sp.wait_ge(hg_mult, hg_count(PAIRS - 1, 9) + 1)
            for w in range(4):
                sp.wait_ge(spilled[w], 16 * (U_G // 4 + 1))
            sp.dma_start(g_hg[:].rearrange("p (u b) t -> p u (b t)", b=2),
                         scratch[U_G:U_G + 4].rearrange("u p c -> p u c")).then_inc(g_back, 16)
            loads(HG_END + 1, HG_END + 10)
            sp.wait_ge(yh_l, 1)
            for k, (unit, dst) in enumerate(((U_QM, q_mem[:].rearrange("p (u b) t -> p u (b t)", b=2)),
                                             (U_KM, k_mem[:].rearrange("p (u b) t -> p u (b t)", b=2)),
                                             (U_VM, v_mem[:].rearrange("p j t c -> p (j t) c")))):
                sp.dma_start(dst, scratch[unit:unit + 4].rearrange("u p c -> p u c")).then_inc(mem_back, 16)
                load(Nth(HG_END + 10 + k))
            first = FIRST["branch"]
            loads(HG_END + 13, first)
            with sp.Fori(0, 2) as i:
                for cg in range(4):
                    for b in range(3):
                        load(Nth(first + 3 * cg + b, i, 12))
                        if b == 1:
                            if cg == 0:
                                sp.wait_ge(valued, UNITS_ATTN)
                            if cg < 2:
                                for w in range(4):
                                    sp.wait_ge(spilled[w], 16 * (UNITS // 4 - 1 + cg))
                            wait_taken(sp, Nth(GROUP["branch"] + 3 * (cg - 2) + 2, i, 12))
                            sp.dma_start(gate[:, cg % 2, :, :],
                                         scratch[bass.ds(i * 12 + (U_GATES + 3 * cg), 3)]
                                         .rearrange("u p c -> p u c")).then_inc(gate_full[cg % 2], 16)
            first = FIRST["w_o"]
            loads(first, first + 4)
            sp.wait_ge(merged_l, 8)
            sp.wait_ge(h_saved, 32)
            for c in range(4):
                part = slice(c * 512, (c + 1) * 512)
                sp.dma_start(z[:, :, part], h_scratch.rearrange("(t p) d -> p t d", p=P)[:, :, part])\
                    .then_inc(z_in[c], 16)
                load(Nth(first + 4 + c))
            for r in range(2):
                gain_and_bias(ln1_rows, 2, r, rows1_in)
                load(Nth(first + 8 + r))
            loads(first + 10, FIRST["down"] + 4)
            sp.wait_ge(piece_used, FIRST["down"])
            for r in range(2):
                gain_and_bias(ln2_rows, 4, r, rows2_in)
                load(Nth(FIRST["down"] + 4 + r))
            loads(FIRST["down"] + 6, PIECES)
            for t in range(TT):
                for c in range(4):
                    part = slice(c * 512, (c + 1) * 512)
                    sp.wait_ge(out_rows, 4 * t + c + 1)
                    sp.dma_start(out[t * P:(t + 1) * P, part], z[:, t, part]).then_inc(out_done, 16)
            sp.wait_ge(out_done, 16 * 4 * TT)

        @block.gpsimd
        def _(pool):
            pool.memset(ones[:], 1.0).then_inc(ones_set, 1)

            def hg_pack_k(p, s):
                k = hg_count(p, s)
                dst = k_hat[:, k % 2]
                if s in (10, 12):
                    return
                if k >= 2:
                    pool.wait_ge(hg_mult, k - 1)
                if s == 11:
                    pool.wait_ge(hg_taken, hg_count(p, 9) + 1)
                    o = q_hg[:, 2 * p:2 * p + 2, :]
                    pool.tensor_tensor(dst, o, o, ALU.mult).then_inc(hg_packed_k, 1)
                    return
                if s == 9:
                    return
                pool.wait_ge(hg_made, 8 * p + max(s, 1))
                if s == 0:
                    pool.tensor_tensor(dst, pre_c[:], pre_d[:], ALU.add).then_inc(hg_packed_k, 1)
                    return
                w = 1 << (s - 1)
                for hand, src in ((0, pre_c), (1, pre_d)):
                    last = pool.tensor_copy(
                        dst.rearrange("p h (b e c) -> p (h b) e c", e=2, c=w)[:, :, hand, :],
                        src[:].rearrange("p h (b e c) -> p (h b) e c", e=2, c=w)[:, :, hand, :])
                last.then_inc(hg_packed_k, 1)

            for j in range(2):
                for g in range(2):
                    wait_taken(pool, GROUP["c_q"] + 2 * j + g)
                if j:
                    pool.wait_ge(c_summed, j)
                c = c_raw[:, KR * j:KR * (j + 1), :]
                pool.tensor_tensor(c_sq[:], c, c, ALU.mult).then_inc(c_squared, 1)
            for n in range(HG_SLOT, HG_END + 1):
                now = hg_at(n, 0)
                if now:
                    hg_pack_k(*now)

        @block.scalar
        def _(act):
            steps = [0]

            def chain(ins):
                steps[0] += 1
                ins.then_inc(act_step, 1)
                act.wait_ge(act_step, steps[0])

            def split_hi(n):
                act.wait_ge(raw_full[n.at(4)], (Nth(n.c // 4, n.i, n.step // 4).value() + 1) * 16)
                act.activation(weight_hi[:, n.at(4), :], raw[:, n.at(4), :], ACT.Copy).then_inc(h_ready, 1)

            def ended(n):
                act.wait_ge(piece_used, n.value() if isinstance(n, Nth) else n)

            def spill_group(n, g, unit, token_major=False):
                ended(n)
                for j in range(2 if token_major else 1):
                    w = unit + j
                    if w >= 4:
                        act.wait_ge(spilled[w % 4], 16 * (w // 4))
                    if token_major:
                        src = pair[g % 2][:, j, :]
                        dst = spill[:, w % 4, :]
                    else:
                        src = pair[g % 2][:, :, 0:T]
                        dst = spill[:, w % 4, :].rearrange("p (b t) -> p b t", b=2)
                    ins = act.activation(dst, src, ACT.Copy)
                    if j == (1 if token_major else 0):
                        ins.then_inc(pair_free[g % 2], 1)
                        wait_taken(act, g)
                    else:
                        chain(ins)
                    act.dma_start(scratch[w], spill[:, w % 4, :]).then_inc(spilled[w % 4], 16)

            def take(n, g, dst, func, columns=T):
                ended(n)
                act.activation(dst, pair[g % 2][:, :, 0:columns], func).then_inc(pair_free[g % 2], 1)

            for c in range(8):
                two = slice(2 * c, 2 * c + 2)
                act.wait_ge(mem_in[c], 16)
                act.activation(mem_hi[:, two, :], mem_raw[:, two, :], ACT.Copy).then_inc(mem_h, 1)
                if c in (0, 3):
                    split_hi(Nth(c // 3))
            split_hi(Nth(2))

            def swap_halves(blocks):
                for h in range(2):
                    for r in range(2):
                        to, of = 2 * HALF * h + HALF * r, 2 * HALF * h + HALF * (1 - r)
                        act.dma_start(rope_swapped[to:to + HALF, 0:blocks, :], rope_x[of:of + HALF, 0:blocks, :])\
                            .then_inc(swapped, 16)

            def root(k):
                act.wait_ge(var_ready, k + 1)
                r = rstd[:, k % 2:k % 2 + 1]
                act.activation(r, r, ACT.Sqrt).then_inc(root_ready, 1)

            def turned_part(b, k0):
                act.wait_ge(turned, k0 + b + 1)
                t, k = b // 4, 4 * (b % 4)
                act.activation(act_hi[:, k:k + 4, t * P:(t + 1) * P],
                               turn_bank(b, k0).rearrange("p (k t) -> p k t", k=4), ACT.Copy).then_inc(turned_h, 1)

            def load_table(func):
                act.activation(spare, hgain, func)

            def slot(n):
                split_hi(Nth(n + LOOK))
                if n in (STATS_SLOT, STATS_SLOT + 1):
                    root(n - STATS_SLOT)
                if n == CONST_SLOT:
                    act.wait_ge(lb_diff, 1)
                    act.activation(small[:, 0:32], small[:, 0:32], ACT.Exp).then_inc(lb_exp, 1)
                if n == CONST_SLOT + 1:
                    act.wait_ge(angle, 1)
                    act.activation(cos[:], prob[:, 0, :], ACT.Sin).then_inc(trig, 1)
                    act.activation(sin[:], prob[:, 1, :], ACT.Sin).then_inc(trig, 1)
                if LN_SLOT < n <= LN_SLOT + 4:
                    for b in (2 * (n - 1 - LN_SLOT), 2 * (n - 1 - LN_SLOT) + 1):
                        turned_part(b, 0)
                for name, unit, count in (("mem_k", U_KM, 8), ("q_mem", U_QM, 8), ("g_hg", U_G, 8),
                                          ("gates", U_GATES, 48)):
                    j = n - FIRST[name]
                    if 2 <= j <= count and j % 2 == 0:
                        if name == "q_mem" and j == 2:
                            act.wait_ge(kz_done, 1)
                        spill_group(n, GROUP[name] + j // 2 - 1, unit + j // 2 - 1)
                j = n - FIRST["mem_v"]
                if j in (4, 8):
                    spill_group(n, GROUP["mem_v"] + j // 4 - 1, U_VM + 2 * (j // 4 - 1), True)
                for name, dst, func in (("f_fw", f_fw, ACT.Sigmoid), ("f_bw", f_bw, ACT.Sigmoid),
                                        ("q_hg", q_hg, ACT.Silu)):
                    j = n - FIRST[name]
                    if 2 <= j <= 8 and j % 2 == 0:
                        if name == "f_fw" and j == 2:
                            act.wait_ge(h_saved, 32)
                            act.wait_ge(turned, 8)
                        take(n, GROUP[name] + j // 2 - 1, dst[:, j - 2:j, :], func)
                j = n - FIRST["i_hg"]
                if j in (4, 8):
                    c = j // 4 - 1
                    take(n, GROUP["i_hg"] + c, v_hg[:, :, c * 512:(c + 1) * 512], ACT.Copy, 512)
                j = n - FIRST["c_q"]
                if 2 <= j <= 8 and j % 2 == 0:
                    take(n, GROUP["c_q"] + j // 2 - 1, c_raw[:, j - 2:j, :], ACT.Copy)
                for j in range(2):
                    if n == FIRST["c_q"] + 5 + 4 * j:
                        act.wait_ge(c_var, j + 1)
                        act.activation(c_rs[:], c_rs[:], ACT.Sqrt).then_inc(c_root, 1)
                    if n == FIRST["c_q"] + 6 + 4 * j:
                        act.wait_ge(c_scaled, j + 1)
                        act.activation(c_hi[:, KR * j:KR * (j + 1), :], c_raw[:, KR * j:KR * (j + 1), :], ACT.Copy)\
                           .then_inc(c_hi_done, 1)
                for name, dst in (("uq_nope", q_nope), ("uk", k_nope)):
                    j = n - FIRST[name]
                    if 1 <= j <= 2:
                        for b in range(2):
                            two = 2 * (j - 1) + b
                            take(n, GROUP[name] + two, dst[:, 2 * two:2 * two + 2, :], ACT.Copy)
                if n == FIRST["uq_rope"] + 1:
                    for w in range(4):
                        act.wait_ge(spilled[w], 16 * 2)
                    for b in range(2):
                        take(n, GROUP["uq_rope"] + b, rope_x[:, 2 * b:2 * b + 2, :], ACT.Copy)
                        wait_taken(act, GROUP["uq_rope"] + b)
                    swap_halves(4)
                j = n - FIRST["uv"]
                if 1 <= j <= 2:
                    take(n, GROUP["uv"] + j - 1, v_mla[:, :, (j - 1) * 512:j * 512], ACT.Copy, 512)
                if n == FIRST["k_rope"] + 1:
                    act.wait_ge(q_rotated, 1)
                    ended(n)
                    g = GROUP["k_rope"]
                    act.activation(rope_x[:, 0, :], pair[g % 2][:, 0, 0:T], ACT.Copy).then_inc(pair_free[g % 2], 1)
                    wait_taken(act, g)
                    swap_halves(1)
                now = hg_at(n, 0)
                if now and now[1] <= 8:
                    p, s = now
                    k = hg_count(p, s)
                    act.wait_ge(hg_made, 8 * p + max(s, 1))
                    if k >= 2:
                        act.wait_ge(hg_mult, k - 1)
                    if s == 0:
                        last = act.activation(q_hat[:, k % 2], q_hg[:, 2 * p:2 * p + 2, :], ACT.Copy)
                    else:
                        w = 1 << (s - 1)
                        for hand, src in ((0, pre_b), (1, pre_a)):
                            last = act.activation(
                                q_hat[:, k % 2].rearrange("p h (b e c) -> p (h b) e c", e=2, c=w)[:, :, hand, :],
                                src[:].rearrange("p h (b e c) -> p (h b) e c", e=2, c=w)[:, :, hand, :], ACT.Copy)
                    last.then_inc(hg_packed_q, 1)
                now = hg_at(n, 3)
                if now and now[1] == 11:
                    act.wait_ge(hg_taken, hg_count(*now) + 1)
                    act.activation(hg_rs[:], hg_rs[:], ACT.Sqrt).then_inc(hg_root, 1)
                if n == HG_END + 2:
                    act.wait_ge(g_back, 16)
                    act.activation(g_hg[:], g_hg[:], ACT.Sigmoid).then_inc(g_open, 1)
                if n == HG_END + 4:
                    act.wait_ge(hg_gated, 1)
                    act.activation(yh_hi[:], q_hg[:], ACT.Copy).then_inc(yh_h, 1)
                attention(n)

            def attention(n):
                u = unit_at(n, 1)
                if u is not None:
                    act.wait_ge(maxed, u + 1)
                    if u >= 1:
                        act.wait_ge(p_turned, u)
                    scale = MLA_SCALE if u < HEADS else MEM_SCALE
                    for t in range(TT):
                        last = act.activation(prob[:, t, :], side[2][:, t * T:(t + 1) * T], ACT.Exp,
                                              bias=row_max[:, t:t + 1], scale=scale,
                                              accum_out=row_sum[:, t:t + 1])
                    last.then_inc(exped, 1)
                u = unit_at(n, 3)
                if u is not None:
                    act.wait_ge(p_turned, u + 1)
                    if u >= 1:
                        act.wait_ge(valued, u)
                    act.activation(prob_t[:], side[3][:].rearrange("p (k t) -> p k t", k=2), ACT.Copy)\
                       .then_inc(pt_done, 1)
                u = unit_at(n, 4)
                if u is not None:
                    act.wait_ge(valued, u + 1)
                    if u < HEADS:
                        act.activation(ym_hi[:, u, :], side[3][:, 0:T], ACT.Copy).then_inc(y_h, 1)
                    else:
                        b = 2 * (u - HEADS)
                        act.activation(yc_hi[:, b:b + 2, :], side[3][:].rearrange("p (k t) -> p k t", k=2), ACT.Copy)\
                           .then_inc(y_h, 1)

            for n in range(1, FIRST["branch"]):
                slot(n)
            n = FIRST["branch"]
            split_hi(Nth(n + LOOK))
            spill_group(n, GROUP["gates"] + 23, UNITS - 1)
            with act.Fori(0, 2) as i:
                load_table(ACT.Sigmoid)
                for cg in range(4):
                    for b in range(3):
                        if b == 0:
                            act.wait_ge(gate_full[cg % 2], (i * 2 + (cg // 2 + 1)) * 16)
                            act.activation(gate[:, cg % 2], gate[:, cg % 2], ACT.Sigmoid).then_inc(gates_open, 1)
                        split_hi(Nth(n + 1 + LOOK + 3 * cg + b, i, 12))
                        if b == 2:
                            act.wait_ge(merged_sum, i * 4 + (cg + 1))
                            act.activation(act_hi[:, bass.ds(i * 8 + 2 * cg, 2), :],
                                           merged[:, cg % 2, :].rearrange("p (b t) -> p b t", b=2), ACT.Copy)\
                               .then_inc(merged_h, 1)
            n = FIRST["w_o"]
            with act.Fori(0, 3) as i:
                for j in range(4):
                    split_hi(Nth(n + 1 + LOOK + j, i, 4))

            split_hi(Nth(n + 15))
            load_table(ACT.Sqrt)
            root(2)
            split_hi(Nth(n + 16))
            for b in (0, 1, 2, 3):
                turned_part(b, 8)
            root(3)
            load_table(ACT.Silu)
            split_hi(Nth(n + 17))
            for b in (4, 5, 6, 7):
                turned_part(b, 8)
            split_hi(Nth(n + 18))
            n = FIRST["ffn"]
            with act.Fori(0, 22) as i:
                load_table(ACT.Silu)
                for j in range(4):
                    split_hi(Nth(n + 1 + LOOK + j, i, 4))
                    if j == 1:
                        g = GROUP["ffn"]
                        ended(Nth(n + 2, i, 4))
                        wait_taken(act, Nth(g - 1, i, 2))
                        act.activation(silu[:].rearrange("p (b t) -> p b t", b=2), pair[g % 2][:, :, 0:T], ACT.Silu)\
                           .then_inc(pair_free[g % 2], 1)
                    if j == 3:
                        wait_taken(act, Nth(g + 1, i, 2))
                        act.activation(ff_hi[:, bass.ds(i * 2, 2), :], ff[:].rearrange("p (b t) -> p b t", b=2),
                                       ACT.Copy).then_inc(ff_h, 1)
            n = FIRST["down"]
            for m in range(n + 1 + LOOK, PIECES):
                split_hi(Nth(m))
            load_table(ACT.Sqrt)
            for k in (4, 5):
                root(k)

        @block.vector
        def _(dve):
            steps = [0]

            def chain(ins):
                steps[0] += 1
                ins.then_inc(dve_step, 1)
                dve.wait_ge(dve_step, steps[0])

            def split_lo(n):
                dve.wait_ge(h_ready, (n + 1).value())
                dve.tensor_tensor(weight_lo[:, n.at(4), :], raw[:, n.at(4), :], weight_hi[:, n.at(4), :].bitcast(F32),
                                  ALU.subtract).then_inc(l_ready, 1)

            for c in range(8):
                dve.wait_ge(mem_h, c + 1)
                two = slice(2 * c, 2 * c + 2)
                dve.tensor_tensor(mem_lo[:, two, :], mem_raw[:, two, :], mem_hi[:, two, :].bitcast(F32), ALU.subtract)\
                   .then_inc(mem_l, 1)
                if c in (0, 3):
                    split_lo(Nth(c // 3))
            split_lo(Nth(2))

            def part_stats(t, c, src):
                return dve.bn_stats(stats[:, t, c, :], src[:, t, c * 512:(c + 1) * 512])

            def row_stats(k, last):
                t = k % 2
                chain(last)
                chain(dve.bn_aggr(mv[:, t, :], stats[:, t, :, :].rearrange("p c k -> p (c k)")))
                dve.tensor_scalar(rstd[:, t:t + 1], mv[:, t, 1:2], LN_EPS, None, ALU.add).then_inc(var_ready, 1)

            def invert_root(k):
                dve.wait_ge(root_ready, k + 1)
                r = rstd[:, k % 2:k % 2 + 1]
                chain(dve.reciprocal(r, r))

            def norm_part(t, c, src, rows, done):
                part = slice(c * 512, (c + 1) * 512)
                v = src[:, t, part]
                chain(dve.scalar_tensor_tensor(out=v, in0=v, scalar=mv[:, t, 0:1], in1=rows[:, 0, part],
                                               op0=ALU.subtract, op1=ALU.mult))
                dve.scalar_tensor_tensor(out=v, in0=v, scalar=rstd[:, t:t + 1], in1=rows[:, 1, part], op0=ALU.mult,
                                         op1=ALU.add).then_inc(done, 1)

            def lo_of_turned(b, k0):
                t, k = b // 4, 4 * (b % 4)
                dve.wait_ge(turned_h, k0 + b + 1)
                dve.tensor_tensor(act_lo[:, k:k + 4, t * P:(t + 1) * P],
                                  turn_bank(b, k0).rearrange("p (k t) -> p k t", k=4),
                                  act_hi[:, k:k + 4, t * P:(t + 1) * P].bitcast(F32), ALU.subtract)\
                   .then_inc(turned_l, 1)

            def lower_bounds(first):
                if first:
                    dve.wait_ge(const_in, 16 * 7)
                    chain(dve.tensor_tensor(lb_max, lbl[:, :, 0, :], lbl[:, :, 1, :], ALU.max))
                    for layer in range(2):
                        ins = dve.tensor_tensor(lbl[:, :, layer, :], lbl[:, :, layer, :], lb_max, ALU.subtract)
                    ins.then_inc(lb_diff, 1)
                else:
                    dve.wait_ge(lb_exp, 1)
                    chain(dve.tensor_tensor(lb_max, lbl[:, :, 0, :], lbl[:, :, 1, :], ALU.add))
                    chain(dve.reciprocal(lb_max, lb_max))
                    chain(dve.tensor_tensor(lb, lbl[:, :, 0, :], lb_max, ALU.mult))
                    chain(dve.tensor_scalar(lb_rest, lb, -1.0, 1.0, ALU.mult, ALU.add))

            def angles():
                a, turns, r = sin[:], prob[:, 0, :], prob[:, 1, :]
                chain(dve.tensor_copy(a, cos[:].bitcast(I32)))
                chain(dve.tensor_scalar(a, a, invf, None, ALU.mult))
                chain(dve.tensor_scalar(turns, a, float(1 / (2 * np.pi)), ROUND, ALU.mult, ALU.add))
                chain(dve.tensor_scalar(turns, turns, ROUND, None, ALU.subtract))
                chain(dve.scalar_tensor_tensor(out=r, in0=turns, scalar=-PI_A, in1=a, op0=ALU.mult, op1=ALU.add))
                chain(dve.scalar_tensor_tensor(out=a, in0=turns, scalar=-PI_B, in1=r, op0=ALU.mult, op1=ALU.add))
                chain(dve.scalar_tensor_tensor(out=r, in0=turns, scalar=-float(PI_C), in1=a, op0=ALU.mult, op1=ALU.add))
                chain(dve.tensor_scalar(r, r, 3.1415925, -3.1415925, ALU.min, ALU.max))
                chain(dve.scalar_tensor_tensor(out=turns, in0=r, scalar=-1.0, in1=r, op0=ALU.mult, op1=ALU.max))
                dve.tensor_scalar(turns, turns, -1.0, float(np.pi / 2), ALU.mult, ALU.add).then_inc(angle, 1)

            def rotate(dst, blocks, k):
                dve.wait_ge(swapped, 64 * (k + 1))
                c, s = (a[:].rearrange("p (o t) -> p o t", o=1).to_broadcast([P, blocks, T]) for a in (cos, sin))
                x, other = rope_x[:, 0:blocks, :], rope_swapped[:, 0:blocks, :]
                dve.tensor_tensor(x, x, c, ALU.mult)
                dve.tensor_tensor(other, other, s, ALU.mult).then_inc(rope_turned, 1)
                dve.wait_ge(rope_turned, k + 1)
                return dve.scalar_tensor_tensor(out=dst, in0=other, scalar=rope_sign, in1=x, op0=ALU.mult, op1=ALU.add)

            def hg_make(p, s):
                if s > 8:
                    return
                hs = slice(2 * p, 2 * p + 2)
                k = 9 * p + s
                if k:
                    dve.wait_ge(hg_packed_q, k)
                    dve.wait_ge(hg_packed_k, k + p - (s == 0))
                if s == 0:
                    if p == 0:
                        for g in (2, 3):
                            wait_taken(dve, GROUP["q_hg"] + g)
                        dve.wait_ge(f_done, 8)
                    dve.tensor_scalar(pre_c[:], f_fw[:, hs, :], -1.0, 1.0, ALU.mult, ALU.add)
                    dve.tensor_scalar(pre_d[:], f_bw[:, hs, :], -1.0, 1.0, ALU.mult, ALU.add)
                    dve.tensor_tensor(pre_a[:], q_hg[:, hs, :], f_fw[:, hs, :], ALU.mult)
                    dve.tensor_tensor(pre_b[:], q_hg[:, hs, :], f_bw[:, hs, :], ALU.mult).then_inc(hg_made, 1)
                    return
                if s == 1:
                    return
                w = 1 << (s - 2)
                n = T // (2 * w)
                dve.wait_ge(hg_made, 8 * p + s - 1)

                def totals(tot, f):
                    if s == 2:
                        return f[:, hs, :].rearrange("p h (b e) -> p (h b) e", e=2)
                    at_ = 2 * T - 4 * T // w
                    flat = tot[:].rearrange("p h t -> p (h t)")
                    return flat[:, at_:at_ + 2 * T // w].rearrange("p (b e) -> p b e", e=2)

                def blocks(a, hand):
                    return a[:].rearrange("p h (b e c) -> p (h b) e c", e=2, c=w)[:, :, hand, :]

                for a, hand, tot, f in ((pre_a, 1, tot_fw, f_fw), (pre_b, 0, tot_bw, f_bw),
                                        (pre_c, 0, tot_fw, f_fw), (pre_d, 1, tot_bw, f_bw)):
                    by = totals(tot, f)[:, :, 1 - hand:2 - hand].to_broadcast([P, 2 * n, w])
                    last = dve.tensor_tensor(blocks(a, hand), blocks(a, hand), by, ALU.mult)
                if s < 8:
                    at_ = 2 * T - 4 * T // (2 * w)
                    for tot, f in ((tot_fw, f_fw), (tot_bw, f_bw)):
                        pairs = totals(tot, f)
                        flat = tot[:].rearrange("p h t -> p (h t)")
                        last = dve.tensor_tensor(flat[:, at_:at_ + 2 * n], pairs[:, :, 0], pairs[:, :, 1], ALU.mult)
                last.then_inc(hg_made, 1)

            def hg_take(p, s):
                if s in (10, 12):
                    return
                k = hg_count(p, s)
                bank = side[k % 2]
                dve.wait_ge(hg_mult, k + 1)
                if k:
                    dve.wait_ge(hg_taken, k)
                blocks = bank[:].rearrange("p (h m t) -> p h m t", h=2, m=2)
                if s == 0:
                    dve.tensor_copy(att[:], blocks).then_inc(hg_taken, 1)
                elif s <= 7:
                    mask = masks[:, s - 1:s, :].to_broadcast([P, 4, P])
                    dve.copy_predicated(att[:].rearrange("p h m t -> p (h m) t"), mask,
                                        bank[:].rearrange("p (b t) -> p b t", b=4)).then_inc(hg_taken, 1)
                elif s == 8:
                    dve.tensor_copy(att_x[:], blocks).then_inc(hg_taken, 1)
                elif s == 9:
                    dve.tensor_copy(q_hg[:, 2 * p:2 * p + 2, :], bank[:].rearrange("p (h t) -> p h t", h=2))\
                       .then_inc(hg_taken, 1)
                else:
                    dve.tensor_scalar(hg_rs[:], bank[:].rearrange("p (h t) -> p h t", h=2), 1.0 / P, RMS_EPS, ALU.mult,
                                      ALU.add).then_inc(hg_taken, 1)

            def hg_norm(p):
                dve.wait_ge(hg_root, p + 1)
                chain(dve.reciprocal(hg_rs[:], hg_rs[:]))
                o = q_hg[:, 2 * p:2 * p + 2, :]
                dve.scalar_tensor_tensor(out=o, in0=o, scalar=hgain, in1=hg_rs[:], op0=ALU.mult, op1=ALU.mult)\
                   .then_inc(hg_normed, 1)

            def attention(n):
                u = unit_at(n, 1)
                if u is not None:
                    dve.wait_ge(scored, u + 1)
                    if u >= 1:
                        dve.wait_ge(exped, u)
                    chain(dve.reduce_max(row_max, side[2][:].rearrange("p (t k) -> p t k", t=2), mybir.AxisListType.X))
                    scale = MLA_SCALE if u < HEADS else MEM_SCALE
                    dve.tensor_scalar(row_max, row_max, -scale, None, ALU.mult).then_inc(maxed, 1)
                u = unit_at(n, 2)
                if u is not None:
                    dve.wait_ge(exped, u + 1)
                    chain(dve.reciprocal(row_sum, row_sum))
                    for t in range(TT):
                        last = dve.tensor_scalar(prob[:, t, :], prob[:, t, :], row_sum[:, t:t + 1], None, ALU.mult)
                    last.then_inc(p_done, 1)

            def attention_lo(n):
                u = unit_at(n, 4)
                if u is not None:
                    dve.wait_ge(y_h, u + 1)
                    if u < HEADS:
                        dve.tensor_tensor(ym_lo[:, u, :], side[3][:, 0:T], ym_hi[:, u, :].bitcast(F32), ALU.subtract)\
                           .then_inc(y_l, 1)
                    else:
                        b = 2 * (u - HEADS)
                        dve.tensor_tensor(yc_lo[:, b:b + 2, :], side[3][:].rearrange("p (k t) -> p k t", k=2),
                                          yc_hi[:, b:b + 2, :].bitcast(F32), ALU.subtract).then_inc(y_l, 1)

            def slot(n):
                now = hg_at(n, 0)
                if now:
                    hg_make(*now)
                split_lo(Nth(n + LOOK))
                now = hg_at(n, 2)
                if now:
                    hg_take(*now)
                attention(n)
                now = hg_at(n, 4)
                if now and now[1] == 11:
                    hg_norm(now[0])
                if n in (STATS_SLOT, STATS_SLOT + 1):
                    t = n - STATS_SLOT
                    dve.wait_ge(x_in[t], 16)
                    for c in range(4):
                        last = part_stats(t, c, h_tok)
                    row_stats(t, last)
                if NORM_SLOT <= n < NORM_SLOT + 4:
                    dve.wait_ge(rows_in, 32)
                    t, half = divmod(n - NORM_SLOT, 2)
                    if half == 0:
                        invert_root(t)
                    for c in (2 * half, 2 * half + 1):
                        norm_part(t, c, h_tok, ln0_rows, h_done)
                if n == CONST_SLOT:
                    lower_bounds(True)
                    angles()
                if n == CONST_SLOT + 2:
                    lower_bounds(False)
                if LN_SLOT < n <= LN_SLOT + 4:
                    for b in (2 * (n - 1 - LN_SLOT), 2 * (n - 1 - LN_SLOT) + 1):
                        lo_of_turned(b, 0)
                for d, (name, f) in enumerate((("f_fw", f_fw), ("f_bw", f_bw))):
                    j = n - FIRST[name]
                    if 2 <= j <= 8 and j % 2 == 0:
                        wait_taken(dve, GROUP[name] + j // 2 - 1)
                        for h in (j - 2, j - 1):
                            last = dve.tensor_scalar(f[:, h, :], f[:, h, :], lb_rest[:, d, h:h + 1], lb[:, d, h:h + 1],
                                                     ALU.mult, ALU.add)
                        last.then_inc(f_done, 1)
                for j in range(2):
                    if n == FIRST["c_q"] + 5 + 4 * j:
                        dve.wait_ge(c_summed, j + 1)
                        dve.tensor_scalar(c_rs[:], side[2][:, 0:T], 1.0 / RANK, RMS_EPS, ALU.mult, ALU.add)\
                           .then_inc(c_var, 1)
                    if n == FIRST["c_q"] + 6 + 4 * j:
                        dve.wait_ge(c_root, j + 1)
                        chain(dve.reciprocal(c_rs[:], c_rs[:]))
                        for b in range(KR * j, KR * (j + 1)):
                            last = dve.scalar_tensor_tensor(out=c_raw[:, b, :], in0=c_raw[:, b, :],
                                                            scalar=cgain[:, b:b + 1], in1=c_rs[:],
                                                            op0=ALU.mult, op1=ALU.mult)
                        last.then_inc(c_scaled, 1)
                        s = slice(KR * j, KR * (j + 1))
                        dve.wait_ge(c_hi_done, j + 1)
                        dve.tensor_tensor(c_lo[:, s, :], c_raw[:, s, :], c_hi[:, s, :].bitcast(F32), ALU.subtract)\
                           .then_inc(c_lo_done, 1)
                if n == FIRST["uq_rope"] + 2:
                    for b in range(2):
                        wait_taken(dve, GROUP["uq_rope"] + b)
                    dve.wait_ge(trig, 2)
                    rotate(q_rope[:], 4, 0).then_inc(q_rotated, 1)
                if n == FIRST["k_rope"] + 2:
                    wait_taken(dve, GROUP["k_rope"])
                    rotate(rope_x[:, 1:2, :], 1, 1).then_inc(k_rotated, 1)
                    dve.wait_ge(k_rotated, 1)
                    for h in range(2):
                        last = dve.tensor_scalar(k_rope[:, h, :], rope_x[:, 1, :], head_rows[:, h:h + 1], None, ALU.mult)
                    last.then_inc(kz_done, 1)
                if n == HG_END + 3:
                    dve.wait_ge(g_open, 1)
                    dve.wait_ge(hg_normed, 4)
                    dve.tensor_tensor(q_hg[:], q_hg[:], g_hg[:], ALU.mult).then_inc(hg_gated, 1)
                if n == HG_END + 5:
                    dve.wait_ge(yh_h, 1)
                    dve.tensor_tensor(yh_lo[:], q_hg[:], yh_hi[:].bitcast(F32), ALU.subtract).then_inc(yh_l, 1)
                attention_lo(n)

            for n in range(1, FIRST["branch"]):
                slot(n)
            n = FIRST["branch"]
            split_lo(Nth(n + LOOK))
            g0 = GROUP["branch"]
            with dve.Fori(0, 2) as i:
                for cg in range(4):
                    acc = merged[:, cg % 2, :].rearrange("p (b t) -> p b t", b=2)
                    for b in range(3):
                        j = 3 * cg + b
                        dve.wait_ge(piece_used, (Nth(n + 1 + j, i, 12)).value())
                        if b == 0:
                            dve.wait_ge(gates_open, i * 4 + (cg + 1))
                        src = pair[(g0 + j) % 2][:, :, 0:T]
                        by = gate[:, cg % 2, b, :].rearrange("p (b t) -> p b t", b=2)
                        group = Nth(g0 + j, i, 12)
                        free = pair_free[group.at(2)]
                        if b == 0:
                            dve.tensor_tensor(acc, src, by, ALU.mult).then_inc(free, 1)
                            wait_taken(dve, group)
                            split_lo(Nth(n + 1 + LOOK + j, i, 12))
                        else:
                            prod = product[:].rearrange("p (b t) -> p b t", b=2)
                            dve.tensor_tensor(prod, src, by, ALU.mult).then_inc(free, 1)
                            wait_taken(dve, group)
                            if b == 1:
                                dve.tensor_tensor(acc, acc, prod, ALU.add).then_inc(merge_part, 1)
                                dve.wait_ge(merge_part, i * 4 + (cg + 1))
                                split_lo(Nth(n + 1 + LOOK + j, i, 12))
                            else:
                                dve.tensor_tensor(acc, acc, prod, ALU.add).then_inc(merged_sum, 1)
                                split_lo(Nth(n + 1 + LOOK + j, i, 12))
                                dve.wait_ge(merged_h, i * 4 + (cg + 1))
                                dst = bass.ds(i * 8 + 2 * cg, 2)
                                dve.tensor_tensor(act_lo[:, dst, :], acc, act_hi[:, dst, :].bitcast(F32), ALU.subtract)\
                                   .then_inc(merged_l, 1)
            n = FIRST["w_o"]
            g0 = GROUP["w_o"]

            def residual(g, c):
                zc = z[:, :, c * 512:(c + 1) * 512]
                dve.scalar_tensor_tensor(out=zc, in0=zc, scalar=ALPHA, in1=pair[g % 2][:], op0=ALU.mult, op1=ALU.add)\
                   .then_inc(pair_free[g % 2], 1)
                wait_taken(dve, g)
                for t in range(TT):
                    last = part_stats(t, c, z)
                return last

            def last_residual(g, k):
                t = k % 2
                zc = z[:, t, 3 * 512:4 * 512]
                ins = dve.scalar_tensor_tensor(out=zc, in0=zc, scalar=ALPHA, in1=pair[g % 2][:, t, :], op0=ALU.mult,
                                               op1=ALU.add)
                if t == 0:
                    chain(ins)
                else:
                    ins.then_inc(pair_free[g % 2], 1)
                    wait_taken(dve, g)
                row_stats(k, part_stats(t, 3, z))

            for c in range(3):
                for j in range(4):
                    split_lo(Nth(n + 1 + LOOK + 4 * c + j))
                dve.wait_ge(z_in[c], 16)
                dve.wait_ge(piece_used, n + 4 * c + 4)
                residual(g0 + c, c)
            split_lo(Nth(n + 15))
            dve.wait_ge(z_in[3], 16)
            dve.wait_ge(tile_summed, 1)
            last_residual(g0 + 3, 2)
            dve.wait_ge(rows1_in, 32)
            invert_root(2)
            for c in range(4):
                norm_part(0, c, z, ln1_rows, h_done)
            split_lo(Nth(n + 16))
            dve.wait_ge(piece_used, n + 16)
            last_residual(g0 + 3, 3)
            invert_root(3)
            for c in range(2):
                norm_part(1, c, z, ln1_rows, h_done)
            for b in (0, 1, 4, 5):
                lo_of_turned(b, 8)
            for c in (2, 3):
                norm_part(1, c, z, ln1_rows, h_done)
            split_lo(Nth(n + 17))
            for b in (2, 3, 6, 7):
                lo_of_turned(b, 8)
            split_lo(Nth(n + 18))
            n = FIRST["ffn"]
            g0 = GROUP["ffn"]
            with dve.Fori(0, 22) as i:
                for j in range(4):
                    split_lo(Nth(n + 1 + LOOK + j, i, 4))
                    if j == 3:
                        dve.wait_ge(piece_used, Nth(n + 4, i, 4).value())
                        wait_taken(dve, Nth(g0, i, 2))
                        dve.tensor_tensor(ff[:].rearrange("p (b t) -> p b t", b=2), pair[(g0 + 1) % 2][:, :, 0:T],
                                          silu[:].rearrange("p (b t) -> p b t", b=2), ALU.mult)\
                           .then_inc(pair_free[(g0 + 1) % 2], 1)
                        dve.wait_ge(ff_h, i + 1)
                        dst = bass.ds(i * 2, 2)
                        dve.tensor_tensor(ff_lo[:, dst, :], ff[:].rearrange("p (b t) -> p b t", b=2),
                                          ff_hi[:, dst, :].bitcast(F32), ALU.subtract).then_inc(ff_l, 1)
            n = FIRST["down"]
            g0 = GROUP["down"]
            for m in range(n + 1, PIECES - LOOK):
                split_lo(Nth(m + LOOK))
                if (m - n) % 11 == 0:
                    c = (m - n) // 11 - 1
                    dve.wait_ge(piece_used, m)
                    residual(g0 + c, c)
            dve.wait_ge(rows2_in, 32)
            for t in range(TT):
                if t == 0:
                    dve.wait_ge(tile_summed, 2)
                else:
                    dve.wait_ge(piece_used, PIECES)
                last_residual(g0 + 3, 4 + t)
                invert_root(4 + t)
                for c in range(4):
                    norm_part(t, c, z, ln2_rows, out_rows)

        @block.tensor
        def _(pe):
            def begin(n):
                pe.wait_ge(l_ready, n.value() + 1)

            def begin_group(g):
                g = g if isinstance(g, Nth) else Nth(g)
                if g.c >= 2:
                    wait_taken(pe, g + -2)

            def features(n, out, width, column, kts, k0, hi, lo, first, last, parts=None):
                w_hi = weight_hi[:, n.at(4), :].rearrange("p (k c) -> p k c", c=width)
                w_lo = weight_lo[:, n.at(4), :].rearrange("p (k c) -> p k c", c=width)
                for k in range(kts):
                    f = slice(column, column + P)
                    a = k0 + k
                    if parts and k % 2 == 0:
                        pe.wait_ge(parts, a // 2 + 1)
                    pe.matmul(out, w_hi[:, k, f], hi[:, a, :], start=first and k == 0, stop=False)
                    pe.matmul(out, w_hi[:, k, f], lo[:, a, :], start=False, stop=False)
                    mm = pe.matmul(out, w_lo[:, k, f], hi[:, a, :], start=False, stop=last and k == kts - 1)
                return mm

            def tokens(n, g, k0, hi, lo, first, last, tiles=(0, 1)):
                w_hi = weight_hi[:, n.at(4), :].rearrange("p (k c) -> p k c", c=512)
                w_lo = weight_lo[:, n.at(4), :].rearrange("p (k c) -> p k c", c=512)
                begin(n)
                for t in tiles:
                    out = pair[g % 2][:, t, :]
                    for k in range(4):
                        tok = slice(t * P, (t + 1) * P)
                        pe.matmul(out, hi[:, k0 + k, tok], w_hi[:, k, :], start=first and k == 0, stop=False)
                        pe.matmul(out, hi[:, k0 + k, tok], w_lo[:, k, :], start=False, stop=False)
                        mm = pe.matmul(out, lo[:, k0 + k, tok], w_hi[:, k, :], start=False, stop=last and k == 3)
                return mm

            def f_piece(n, g, half, hi, lo, halves=2, parts=None, between=None):
                begin(n)
                if half == 0:
                    begin_group(g)
                for b in range(2):
                    mm = features(n, pair[g.at(2)][:, b, 0:T], 256, b * P, 8, 8 * half, hi, lo, half == 0,
                                  half == halves - 1, parts if b == 0 else None)
                    if b == 0 and between:
                        between()
                mm.then_inc(piece_used, 1)

            def t_piece(n, g, quarter, quarters, hi, lo):
                if quarter == 0:
                    begin_group(g)
                tokens(n, g, 4 * quarter, hi, lo, quarter == 0, quarter == quarters - 1).then_inc(piece_used, 1)

            def tile_by_tile(n, g, count, quarters, hi, lo, between=None):
                for t in range(TT):
                    for q in range(quarters - count, quarters):
                        m = n - quarters + q
                        mm = tokens(Nth(m), g, 4 * q, hi, lo, q == 0, q == quarters - 1, (t,))
                        if t == 1:
                            mm.then_inc(piece_used, 1)
                            if between:
                                between(q)
                    if t == 0:
                        mm.then_inc(tile_summed, 1)

            def four_blocks(n, g, hi, lo, k0):
                begin(n)
                for b in range(4):
                    if b % 2 == 0:
                        begin_group(g + b // 2)
                    mm = features(n, pair[(g + b // 2) % 2][:, b % 2, 0:T], 512, b * P, 4, k0, hi, lo, True, True)
                mm.then_inc(piece_used, 1)

            def turn(b, src, k0, rows):
                t, k = b // 4, 4 * (b % 4)
                if b == 0 and not k0:
                    pe.wait_ge(ident_in, 16)
                pe.wait_ge(rows, k0 + b + 1)
                if k0 and b in (4, 5):
                    wait_taken(pe, GROUP["w_o"] + 3)
                elif b >= 4:
                    pe.wait_ge(turned_l, k0 + b - (5 if k0 else 3))
                for j in range(4):
                    mm = pe.transpose(turn_bank(b, k0)[:, j * P:(j + 1) * P], src[:, t, (k + j) * P:(k + j + 1) * P],
                                      ident[:])
                mm.then_inc(turned, 1)

            def hg_multiply(p, s):
                if s in (10, 12):
                    return
                k = hg_count(p, s)
                bank = side[k % 2]
                if k >= 2:
                    pe.wait_ge(hg_taken, k - 1)
                if s <= 8:
                    pe.wait_ge(hg_packed_q, 9 * p + s + 1)
                    pe.wait_ge(hg_packed_k, 10 * p + s + 1)
                    for h in range(2):
                        for m in range(TT):
                            keys = m if s < 8 else 1 - m
                            mm = pe.matmul(bank[:, (2 * h + m) * P:(2 * h + m + 1) * P],
                                           k_hat[:, k % 2, h, keys * P:(keys + 1) * P],
                                           q_hat[:, k % 2, h, m * P:(m + 1) * P], start=True, stop=True)
                elif s == 9:
                    pe.wait_ge(hg_taken, k)
                    for h in range(2):
                        for m in range(TT):
                            o = bank[:, (2 * h + m) * P:(2 * h + m + 1) * P]
                            v = slice((2 * p + h) * VD, (2 * p + h + 1) * VD)
                            pe.matmul(o, v_hg[:, m, v], att[:, h, m, :], start=True, stop=False)
                            mm = pe.matmul(o, v_hg[:, 1 - m, v], att_x[:, h, m, :], start=False, stop=True)
                else:
                    pe.wait_ge(hg_packed_k, 10 * (p + 1))
                    mm = pe.matmul(bank[:], ones[:], k_hat[:, k % 2].rearrange("p h t -> p (h t)"), start=True,
                                   stop=True)
                mm.then_inc(hg_mult, 1)

            def attention(n):
                u = unit_at(n, 2)
                if u is not None:
                    pe.wait_ge(p_done, u + 1)
                    if u >= 1:
                        pe.wait_ge(y_l, u)
                    for k in range(2):
                        for t in range(TT):
                            at_ = k * T + t * P
                            mm = pe.transpose(side[3][:, at_:at_ + P], prob[:, t, k * P:(k + 1) * P], ident[:])
                    mm.then_inc(p_turned, 1)
                u = unit_at(n, 3)
                if u is not None:
                    pe.wait_ge(pt_done, u + 1)
                    if u < HEADS:
                        for k in range(2):
                            mm = pe.matmul(side[3][:, 0:T], v_mla[:, k, u * VD:(u + 1) * VD], prob_t[:, k, :],
                                           start=k == 0, stop=k == 1)
                    else:
                        for b in range(2):
                            f = (2 * (u - HEADS) + b) * P
                            for k in range(2):
                                mm = pe.matmul(side[3][:, b * T:(b + 1) * T],
                                               v_mem[:, f // 512, k, f % 512:f % 512 + P], prob_t[:, k, :],
                                               start=k == 0, stop=k == 1)
                    mm.then_inc(valued, 1)
                u = unit_at(n, 0)
                if u is not None:
                    if u == 0:
                        pe.wait_ge(kz_done, 1)
                        pe.wait_ge(c_var, 2)
                    else:
                        pe.wait_ge(exped, u)
                    if u == HEADS:
                        pe.wait_ge(mem_back, 48)
                    for t in range(TT):
                        out, tok = side[2][:, t * T:(t + 1) * T], slice(t * P, (t + 1) * P)
                        if u < HEADS:
                            pe.matmul(out, q_nope[:, u, tok], k_nope[:, u, :], start=True, stop=False)
                            mm = pe.matmul(out, q_rope[:, u // 2, tok], k_rope[:, u % 2, :], start=False, stop=True)
                        else:
                            for j in range(2):
                                b = 2 * (u - HEADS) + j
                                mm = pe.matmul(out, q_mem[:, b, tok], k_mem[:, b, :], start=j == 0, stop=j == 1)
                    mm.then_inc(scored, 1)

            def after(n):
                if LN_SLOT <= n < LN_SLOT + 4:
                    for b in (2 * (n - LN_SLOT), 2 * (n - LN_SLOT) + 1):
                        turn(b, h_tok, 0, h_done)
                for j in range(2):
                    if n == FIRST["c_q"] + 4 + 4 * j:
                        pe.wait_ge(ones_set, 1)
                        pe.wait_ge(c_squared, j + 1)
                        if j:
                            pe.wait_ge(c_var, j)
                        for b in range(KR):
                            mm = pe.matmul(side[2][:, 0:T], ones[:], c_sq[:, b, :], start=b == 0, stop=b == KR - 1)
                        mm.then_inc(c_summed, 1)
                now = hg_at(n, 1)
                if now:
                    hg_multiply(*now)
                attention(n)

            def f_phase(name, count, hi, lo):
                for j in range(count):
                    n = FIRST[name] + j
                    parts = mem_l if name == "mem_k" and j < 2 else None
                    f_piece(Nth(n), Nth(GROUP[name] + j // 2), j % 2, hi, lo, parts=parts)
                    after(n)

            def t_phase(name, count, quarters, hi, lo):
                for j in range(count):
                    n = FIRST[name] + j
                    if name == "w_o" and j < quarters:
                        pe.wait_ge(merged_l, 2 * j + 2)
                    if name == "down" and j < quarters:
                        pe.wait_ge(ff_l, 2 * j + 2)
                    t_piece(Nth(n), GROUP[name] + j // quarters, j % quarters, quarters, hi, lo)
                    after(n)

            f_phase("mem_k", 8, mem_hi, mem_lo)
            t_phase("mem_v", 8, 4, mem_hi, mem_lo)
            pe.wait_ge(turned_l, 8)
            f_phase("c_q", 4, act_hi, act_lo)
            f_phase("c_kv", 4, act_hi, act_lo)
            f_piece(Nth(FIRST["f_fw"]), Nth(GROUP["f_fw"]), 0, act_hi, act_lo)
            after(FIRST["f_fw"])
            f_piece(Nth(FIRST["f_fw"] + 1), Nth(GROUP["f_fw"]), 1, act_hi, act_lo)
            f_piece(Nth(FIRST["f_fw"] + 2), Nth(GROUP["f_fw"] + 1), 0, act_hi, act_lo)
            f_piece(Nth(FIRST["f_fw"] + 3), Nth(GROUP["f_fw"] + 1), 1, act_hi, act_lo)
            with pe.Fori(0, 5) as i:
                for j in range(4):
                    f_piece(Nth(FIRST["f_fw"] + 4 + j, i, 4), Nth(GROUP["f_fw"] + 2 + j // 2, i, 2), j % 2, act_hi,
                            act_lo)
            t_phase("i_hg", 8, 4, act_hi, act_lo)
            for name, c in (("uq_nope", 0), ("uq_rope", 0), ("uk", 1)):
                pe.wait_ge(c_lo_done, c + 1)
                for j in range(GROUPS[name] // 2):
                    n = FIRST[name] + j
                    four_blocks(Nth(n), GROUP[name] + 2 * j, c_hi, c_lo, KR * c)
                    after(n)
            for j in range(2):
                n = FIRST["uv"] + j
                begin_group(GROUP["uv"] + j)
                tokens(Nth(n), GROUP["uv"] + j, KR, c_hi, c_lo, True, True).then_inc(piece_used, 1)
                after(n)
            begin_group(GROUP["k_rope"])
            n = Nth(FIRST["k_rope"])
            begin(n)
            features(n, pair[GROUP["k_rope"] % 2][:, 0, 0:T], P, 0, KD, 0, act_hi, act_lo, True, True)\
                .then_inc(piece_used, 1)
            after(n.c)
            f_phase("q_mem", 8, act_hi, act_lo)
            f_phase("g_hg", 8, act_hi, act_lo)
            f_phase("gates", 48, act_hi, act_lo)
            pe.wait_ge(yh_l, 1)
            pe.wait_ge(y_l, UNITS_ATTN)
            with pe.Fori(0, 2) as i:
                for j in range(12):
                    hi, lo = ((yh_hi, yh_lo), (ym_hi, ym_lo), (yc_hi, yc_lo))[j % 3]
                    f_piece(Nth(FIRST["branch"] + j, i, 12), Nth(GROUP["branch"] + j, i, 12), 0, hi, lo, 1)
            t_phase("w_o", 12, 4, act_hi, act_lo)

            def turn_first_tile(q):
                if q >= 2:
                    for b in (2 * q - 4, 2 * q - 3):
                        turn(b, z, 8, h_done)

            begin_group(GROUP["w_o"] + 3)
            tile_by_tile(FIRST["w_o"] + 16, GROUP["w_o"] + 3, 4, 4, act_hi, act_lo, turn_first_tile)
            def turn_second_tile(*bs):
                for b in bs:
                    turn(b, z, 8, h_done)

            turn_second_tile(4, 5)
            pe.wait_ge(turned_l, 12)
            f_piece(Nth(FIRST["ffn"]), Nth(GROUP["ffn"]), 0, act_hi, act_lo, between=lambda: turn_second_tile(6, 7))
            pe.wait_ge(turned_l, 16)
            for j in range(1, 4):
                f_piece(Nth(FIRST["ffn"] + j), Nth(GROUP["ffn"] + j // 2), j % 2, act_hi, act_lo)
            with pe.Fori(1, 22) as i:
                for j in range(4):
                    f_piece(Nth(FIRST["ffn"] + j, i, 4), Nth(GROUP["ffn"] + j // 2, i, 2), j % 2, act_hi, act_lo)
            t_phase("down", 41, 11, ff_hi, ff_lo)
            tile_by_tile(PIECES, GROUP["down"] + 3, 3, 11, ff_hi, ff_lo)


def _pieces(inputs):
    w_in, w_uq, w_ukv = inputs["w_in"][0], inputs["mla_w_uq"][0], inputs["mla_w_ukv"][0]
    w_mem, w_branch, w_o = inputs["mem_w_kv"][0], inputs["w_branch"][0], inputs["w_o"][0]
    w_gate, w_up, w_down = inputs["w_ffn_gate"][0], inputs["w_ffn_up"][0], inputs["w_ffn_down"][0]
    at, begin = 0, {}
    for name, width in (("q", BW), ("i", BW), ("f_fw", BW), ("f_bw", BW), ("g", BW), ("c_q", RANK), ("c_kv", RANK),
                        ("k_rope", ROPE), ("q_mem", BW), ("gates", 3 * D)):
        begin[name] = at
        at += width

    def cut(w, k0, kts, columns):
        part = w[k0 * P:(k0 + kts) * P]
        part = part[:, columns]
        return part.reshape(kts, P, -1).transpose(1, 0, 2).reshape(P, PIECE)

    def features(w, c0, width):
        for c in range(c0, c0 + width, 256):
            for half in range(2):
                yield cut(w, 8 * half, 8, slice(c, c + 256))

    def tokens(w, c0, width, quarters=4):
        for c in range(c0, c0 + width, 512):
            for q in range(quarters):
                yield cut(w, 4 * q, 4, slice(c, c + 512))

    heads = np.arange(HEADS)
    uq = heads[:, None] * (NOPE + ROPE)
    nope = uq + np.arange(NOPE)
    rope = uq + NOPE + np.arange(ROPE)
    ukv = heads[:, None] * (NOPE + VD)
    yield from features(w_mem, 0, BW)
    yield from tokens(w_mem, BW, BW)
    yield from features(w_in, begin["c_q"], RANK)
    yield from features(w_in, begin["c_kv"], RANK)
    for name in ("f_fw", "f_bw", "q"):
        yield from features(w_in, begin[name], BW)
    yield from tokens(w_in, begin["i"], BW)
    for four in range(2):
        yield cut(w_uq, 0, KR, nope[4 * four:4 * four + 4].ravel())
    yield cut(w_uq, 0, KR, rope.ravel())
    for part in (0, NOPE):
        for four in range(2):
            yield cut(w_ukv, 0, KR, (ukv + part + np.arange(P))[4 * four:4 * four + 4].ravel())
    yield cut(w_in, 0, KD, np.tile(begin["k_rope"] + np.arange(ROPE), 2))
    yield from features(w_in, begin["q_mem"], BW)
    yield from features(w_in, begin["g"], BW)
    for c in range(0, D, 256):
        for b in range(3):
            yield from features(w_in, begin["gates"] + b * D + c, 256)
    for c in range(0, D, 256):
        for b in range(3):
            yield cut(w_branch[b], 0, 8, slice(c, c + 256))
    yield from tokens(w_o, 0, D)
    for c in range(0, DFF, 256):
        yield from features(w_gate, c, 256)
        yield from features(w_up, c, 256)
    yield from tokens(w_down, 0, D, KF // 4)


def kernel(**inputs):
    import concourse.bacc as bacc
    from concourse.bass_utils import run_bass_kernel_spmd

    inputs = {name: np.asarray(a) for name, a in inputs.items()}
    stream = np.empty((PIECES, P, PIECE), np.float32)
    n = 0
    for n, piece in enumerate(_pieces(inputs)):
        stream[n] = piece
    assert n == PIECES - 1

    def per_partition(a):
        return np.ascontiguousarray(np.moveaxis(a.reshape(a.shape[:-1] + (-1, P)), -1, 0).reshape(P, -1))

    bits = np.arange(P)[:, None] ^ np.arange(P)[None, :]
    masks = np.stack([(bits >> level) == 1 for level in range(LEVELS - 1)], axis=1).astype(np.int32)
    arrays = {
        "stream": stream,
        "mem_t": np.ascontiguousarray(inputs["mem"][0].T.reshape(KD, P, T).transpose(1, 0, 2)),
        "x": np.ascontiguousarray(inputs["x"][0]),
        "pos": np.ascontiguousarray(inputs["positions"]),
        "ln_rows": np.stack([inputs["ln_emb_g"], inputs["ln_emb_b"], inputs["ln1_g"][0], inputs["ln1_b"][0],
                             inputs["ln2_g"][0], inputs["ln2_b"][0]]),
        "lb_logits": per_partition(inputs["hgrn_lb_logits"]),
        "hg_gain": np.ascontiguousarray(inputs["hgrn_norm_g"][0][:, None]),
        "c_gains": per_partition(np.stack([inputs["mla_g_cq"][0], inputs["mla_g_ckv"][0]])),
        "inv_freq": np.tile((np.float32(ROPE_THETA) ** (-np.arange(HALF, dtype=np.float32) / np.float32(HALF)))
                            .astype(np.float32), 4)[:, None],
        "identity": np.eye(P, dtype=np.float32),
        "level_masks": masks,
        "head_mask": np.stack([np.tile(np.repeat([-1, 1], HALF), 2), np.repeat([1, 0], ROPE),
                               np.repeat([0, 1], ROPE)], axis=1).astype(np.float32),
    }
    nc = bacc.Bacc("TRN2", target_bir_lowering=False, num_devices=1, dynamic_dma_scratch_size=1024)
    args = [nc.dram_tensor(f"in_{name}", a.shape, mybir.dt.from_np(a.dtype), kind="ExternalInput").ap()
            for name, a in arrays.items()]
    out = nc.dram_tensor("out", (T, D), F32, kind="ExternalOutput").ap()
    encoder_program(nc, *args, out)
    r = run_bass_kernel_spmd(nc, [{f"in_{name}": a for name, a in arrays.items()}], core_ids=[0])
    return r.results[0]["out"].reshape(1, T, D)
```
